# Optimizing a Trainium2 kernel written in Bass

```python
import math
import jax
import jax.numpy as jnp
from jax import lax
import numpy as np
import jax, jax.numpy as jnp

D_MODEL = 1024
BATCH = 1
SEQ = 256
DEPTH = 2

D_MIX = D_MODEL
GROUP_W = D_MIX // 4
HEAD_DIM = 64
GLA_HEADS = GROUP_W // HEAD_DIM
GLA_GATE_RANK = 16
GLA_GATE_NORMALIZER = 16.0
GLA_CHUNK = 64
FOX_HEADS = GROUP_W // HEAD_DIM
FOX_BLOCK = 128
SSM_HEADS = GROUP_W // HEAD_DIM
SSM_HEAD_DIM = HEAD_DIM
SSM_GROUPS = 2
SSM_STATE = 128
SSM_CONV = 4
SSM_CHUNK = 128
SSM_XBC = GROUP_W + 2 * SSM_GROUPS * SSM_STATE
SC_GROUPS = 4
SC_CONV = 3
D_FF = 2816
EPS = 1e-6

GLA_COLS = 4 * GROUP_W + GLA_GATE_RANK
FOX_COLS = 3 * GROUP_W + FOX_HEADS
SSM_COLS = GROUP_W + SSM_XBC + SSM_HEADS
SC_COLS = 3 * GROUP_W
IN_COLS = GLA_COLS + FOX_COLS + SSM_COLS + SC_COLS


def rms_norm(x, g):
    xf = x.astype(jnp.float32)
    y = xf * lax.rsqrt(jnp.mean(xf * xf, axis=-1, keepdims=True) + EPS)
    return (y * g.astype(jnp.float32)).astype(x.dtype)

def headwise_rms(x, g, n):
    shp = x.shape
    y = rms_norm(x.reshape(shp[:-1] + (shp[-1] // n, n)), g.reshape(-1, n))
    return y.reshape(shp)

def swiglu(h, w_gate, w_up, w_down):
    return (jax.nn.silu(h @ w_gate) * (h @ w_up)) @ w_down

def causal_depthwise_conv(u, w):
    K, C = w.shape
    return lax.conv_general_dilated(
        u, w[:, None, :].astype(u.dtype), window_strides=(1,),
        padding=[(K - 1, 0)], dimension_numbers=('NWC', 'WIO', 'NWC'),
        feature_group_count=C)

def gla_mixer(q, k, v, g_out, g_lr, w_gate_up, b_gate, norm_g):
    dtype = q.dtype
    f32 = jnp.float32
    Bsz, L, _ = q.shape
    H, D, C = GLA_HEADS, HEAD_DIM, GLA_CHUNK
    NC = L // C
    log_a = jax.nn.log_sigmoid((g_lr @ w_gate_up + b_gate).astype(f32)) / GLA_GATE_NORMALIZER

    def chunked(t):
        return t.astype(f32).reshape(Bsz, NC, C, H, D)

    qc = chunked(q) * (D ** -0.5)
    kc, vc, gc = chunked(k), chunked(v), chunked(log_a)
    b = jnp.cumsum(gc, axis=2)
    b_last = b[:, :, -1]
    q_dec = qc * jnp.exp(b)
    k_dec = kc * jnp.exp(-b)
    causal = jnp.tril(jnp.ones((C, C), bool))
    att = jnp.einsum('bnihd,bnjhd->bnhij', q_dec, k_dec)
    att = jnp.where(causal, att, 0.0)
    o_intra = jnp.einsum('bnhij,bnjhv->bnihv', att, vc)
    k_to_end = kc * jnp.exp(b_last[:, :, None] - b)
    chunk_kv = jnp.einsum('bnjhd,bnjhv->nbhdv', k_to_end, vc)
    chunk_decay = jnp.exp(b_last).transpose(1, 0, 2, 3)

    def step(S, inp):
        kv, dec = inp
        return S * dec[..., None] + kv, S

    S0 = jnp.zeros((Bsz, H, D, D), f32)
    _, S_prev = lax.scan(step, S0, (chunk_kv, chunk_decay))
    o_inter = jnp.einsum('bnihd,nbhdv->bnihv', q_dec, S_prev)
    o = (o_intra + o_inter).reshape(Bsz, L, H * D)
    o = headwise_rms(o, norm_g, D) * jax.nn.silu(g_out.astype(f32))
    return o.astype(dtype)

def fox_mixer(q, k, v, f_logit, b_forget, q_norm, k_norm, out_norm):
    dtype = q.dtype
    f32 = jnp.float32
    Bsz, L, _ = q.shape
    H, D, T = FOX_HEADS, HEAD_DIM, FOX_BLOCK
    NB = L // T
    qh = rms_norm(q.astype(f32).reshape(Bsz, L, H, D), q_norm) * (D ** -0.5)
    kh = rms_norm(k.astype(f32).reshape(Bsz, L, H, D), k_norm)
    vh = v.astype(f32).reshape(Bsz, L, H, D)
    log_f = jax.nn.log_sigmoid(f_logit.astype(f32) + b_forget.astype(f32))
    F = jnp.cumsum(log_f, axis=1)
    q_blocks = qh.reshape(Bsz, NB, T, H, D).transpose(1, 0, 2, 3, 4)
    F_blocks = F.reshape(Bsz, NB, T, H).transpose(1, 0, 2, 3)
    F_keys = F.transpose(0, 2, 1)[:, :, None, :]
    k_pos = jnp.arange(L)

    def block(args):
        qb, Fb, i = args
        s = jnp.einsum('bqhd,bkhd->bhqk', qb, kh)
        s = s + (Fb.transpose(0, 2, 1)[..., None] - F_keys)
        q_pos = i * T + jnp.arange(T)
        s = jnp.where(k_pos[None, :] <= q_pos[:, None], s, -jnp.inf)
        p = jax.nn.softmax(s, axis=-1)
        return jnp.einsum('bhqk,bkhd->bqhd', p, vh)

    o = lax.map(block, (q_blocks, F_blocks, jnp.arange(NB)))
    o = o.transpose(1, 0, 2, 3, 4).reshape(Bsz, L, H * D)
    return headwise_rms(o, out_norm, D).astype(dtype)

def ssd_mixer(z, xbc, dt_raw, conv_w, conv_b, dt_bias, A_log, D_skip, norm_g):
    dtype = z.dtype
    f32 = jnp.float32
    Bsz, L, _ = z.shape
    H, P, G, N, Q = SSM_HEADS, SSM_HEAD_DIM, SSM_GROUPS, SSM_STATE, SSM_CHUNK
    NC = L // Q
    xbc = jax.nn.silu(causal_depthwise_conv(xbc, conv_w) + conv_b).astype(f32)
    xs = xbc[..., :GROUP_W].reshape(Bsz, L, H, P)
    Bm = jnp.repeat(xbc[..., GROUP_W:GROUP_W + G * N].reshape(Bsz, L, G, N), H // G, axis=2)
    Cm = jnp.repeat(xbc[..., GROUP_W + G * N:].reshape(Bsz, L, G, N), H // G, axis=2)
    dt = jax.nn.softplus(dt_raw.astype(f32) + dt_bias.astype(f32))
    A = -jnp.exp(A_log.astype(f32))
    a = (dt * A).reshape(Bsz, NC, Q, H).transpose(0, 3, 1, 2)
    Xd = (xs * dt[..., None]).reshape(Bsz, NC, Q, H, P)
    Bc = Bm.reshape(Bsz, NC, Q, H, N)
    Cc = Cm.reshape(Bsz, NC, Q, H, N)
    a_cs = jnp.cumsum(a, axis=-1)
    causal = jnp.tril(jnp.ones((Q, Q), bool))
    seg = a_cs[..., :, None] - a_cs[..., None, :]
    Lmat = jnp.exp(jnp.where(causal, seg, -jnp.inf))
    scores = jnp.einsum('bcihn,bcjhn->bhcij', Cc, Bc) * Lmat
    y_diag = jnp.einsum('bhcij,bcjhp->bcihp', scores, Xd)
    decay_to_end = jnp.exp(a_cs[..., -1:] - a_cs)
    chunk_states = jnp.einsum('bcjhn,bhcj,bcjhp->cbhpn', Bc, decay_to_end, Xd)
    chunk_decay = jnp.exp(a_cs[..., -1]).transpose(2, 0, 1)

    def step(S, inp):
        st, dec = inp
        return S * dec[..., None, None] + st, S

    S0 = jnp.zeros((Bsz, H, P, N), f32)
    _, S_prev = lax.scan(step, S0, (chunk_states, chunk_decay))
    y_off = jnp.einsum('bcihn,cbhpn,bhci->bcihp', Cc, S_prev, jnp.exp(a_cs))
    y = (y_diag + y_off).reshape(Bsz, L, H, P) + xs * D_skip.astype(f32)[:, None]
    y = y.reshape(Bsz, L, H * P) * jax.nn.silu(z.astype(f32))
    return headwise_rms(y, norm_g, GROUP_W // G).astype(dtype)

def short_conv_mixer(b_gate, c_gate, val, conv_w, out_norm):
    y = b_gate * causal_depthwise_conv(c_gate * val, conv_w)
    return headwise_rms(y, out_norm, GROUP_W // SC_GROUPS)

def hybrid_mixing(h, w_in, gla_w_gate_up, gla_b_gate, gla_norm,
                  fox_b_forget, fox_q_norm, fox_k_norm, fox_out_norm,
                  ssm_conv_w, ssm_conv_b, ssm_dt_bias, ssm_A_log, ssm_D, ssm_norm,
                  sc_conv_w, sc_out_norm, w_out):
    proj = h @ w_in
    sizes = ([GROUP_W] * 4 + [GLA_GATE_RANK] + [GROUP_W] * 3 + [FOX_HEADS]
             + [GROUP_W, SSM_XBC, SSM_HEADS] + [GROUP_W] * 3)
    cuts = [int(c) for c in np.cumsum(sizes)[:-1]]
    (a_q, a_k, a_v, a_g, a_lr, b_q, b_k, b_v, b_f,
     c_z, c_xbc, c_dt, d_b, d_c, d_v) = jnp.split(proj, cuts, axis=-1)
    y_a = gla_mixer(a_q, a_k, a_v, a_g, a_lr, gla_w_gate_up, gla_b_gate, gla_norm)
    y_b = fox_mixer(b_q, b_k, b_v, b_f, fox_b_forget, fox_q_norm, fox_k_norm, fox_out_norm)
    y_c = ssd_mixer(c_z, c_xbc, c_dt, ssm_conv_w, ssm_conv_b, ssm_dt_bias, ssm_A_log, ssm_D, ssm_norm)
    y_d = short_conv_mixer(d_b, d_c, d_v, sc_conv_w, sc_out_norm)
    y = jnp.concatenate([y_a, y_b, y_c, y_d], axis=-1).astype(h.dtype)
    return y @ w_out

def first_inputs(seed: int = 0) -> dict:
    key = jax.random.key(seed)
    k = jax.random.split(key, 27)
    f32 = jnp.float32
    Ld = DEPTH

    def nrm(kk, shape, scale):
        return jax.random.normal(kk, shape, f32) * scale

    def gain(kk, shape):
        return 1.0 + 0.02 * jax.random.normal(kk, shape, f32)

    dt0 = jnp.exp(jax.random.uniform(k[16], (Ld, SSM_HEADS), f32, math.log(1e-3), math.log(1e-1)))
    return {
        'x': nrm(k[0], (BATCH, SEQ, D_MODEL), 1.0),
        'ffn1_norm': gain(k[1], (Ld, D_MODEL)),
        'ffn1_w_gate': nrm(k[2], (Ld, D_MODEL, D_FF), D_MODEL ** -0.5),
        'ffn1_w_up': nrm(k[3], (Ld, D_MODEL, D_FF), D_MODEL ** -0.5),
        'ffn1_w_down': nrm(k[4], (Ld, D_FF, D_MODEL), D_FF ** -0.5),
        'mix_norm': gain(k[5], (Ld, D_MODEL)),
        'w_in': nrm(k[6], (Ld, D_MODEL, IN_COLS), D_MODEL ** -0.5),
        'gla_w_gate_up': nrm(k[7], (Ld, GLA_GATE_RANK, GROUP_W), GLA_GATE_RANK ** -0.5),
        'gla_b_gate': nrm(k[8], (Ld, GROUP_W), 0.1),
        'gla_norm': gain(k[9], (Ld, GROUP_W)),
        'fox_b_forget': 2.0 + nrm(k[10], (Ld, FOX_HEADS), 0.1),
        'fox_q_norm': gain(k[11], (Ld, HEAD_DIM)),
        'fox_k_norm': gain(k[12], (Ld, HEAD_DIM)),
        'fox_out_norm': gain(k[13], (Ld, GROUP_W)),
        'ssm_conv_w': nrm(k[14], (Ld, SSM_CONV, SSM_XBC), SSM_CONV ** -0.5),
        'ssm_conv_b': nrm(k[15], (Ld, SSM_XBC), 0.02),
        'ssm_dt_bias': dt0 + jnp.log(-jnp.expm1(-dt0)),
        'ssm_A_log': jnp.log(jax.random.uniform(k[17], (Ld, SSM_HEADS), f32, 1.0, 16.0)),
        'ssm_D': 1.0 + nrm(k[18], (Ld, SSM_HEADS), 0.1),
        'ssm_norm': gain(k[19], (Ld, GROUP_W)),
        'sc_conv_w': nrm(k[20], (Ld, SC_CONV, GROUP_W), SC_CONV ** -0.5),
        'sc_out_norm': gain(k[21], (Ld, GROUP_W)),
        'w_out': nrm(k[22], (Ld, D_MIX, D_MODEL), D_MIX ** -0.5),
        'ffn2_norm': gain(k[23], (Ld, D_MODEL)),
        'ffn2_w_gate': nrm(k[24], (Ld, D_MODEL, D_FF), D_MODEL ** -0.5),
        'ffn2_w_up': nrm(k[25], (Ld, D_MODEL, D_FF), D_MODEL ** -0.5),
        'ffn2_w_down': nrm(k[26], (Ld, D_FF, D_MODEL), D_FF ** -0.5),
    }

def first_block(x, ffn1_norm, ffn1_w_gate, ffn1_w_up, ffn1_w_down,
              mix_norm, w_in, gla_w_gate_up, gla_b_gate, gla_norm,
              fox_b_forget, fox_q_norm, fox_k_norm, fox_out_norm,
              ssm_conv_w, ssm_conv_b, ssm_dt_bias, ssm_A_log, ssm_D, ssm_norm,
              sc_conv_w, sc_out_norm, w_out,
              ffn2_norm, ffn2_w_gate, ffn2_w_up, ffn2_w_down):
    for l in range(DEPTH):
        x = x + 0.5 * swiglu(rms_norm(x, ffn1_norm[l]), ffn1_w_gate[l], ffn1_w_up[l], ffn1_w_down[l])
        h = rms_norm(x, mix_norm[l])
        x = x + hybrid_mixing(h, w_in[l], gla_w_gate_up[l], gla_b_gate[l], gla_norm[l],
                              fox_b_forget[l], fox_q_norm[l], fox_k_norm[l], fox_out_norm[l],
                              ssm_conv_w[l], ssm_conv_b[l], ssm_dt_bias[l], ssm_A_log[l],
                              ssm_D[l], ssm_norm[l], sc_conv_w[l], sc_out_norm[l], w_out[l])
        x = x + 0.5 * swiglu(rms_norm(x, ffn2_norm[l]), ffn2_w_gate[l], ffn2_w_up[l], ffn2_w_down[l])
    return x


N_MEM = 256
ATT_GROUPS = ((128, 1), (512, 4), (2048, 16))
N_ATT_GROUPS = len(ATT_GROUPS)
ATT_HEADS = 4
ATT_HEAD_DIM = 128
ATT_WIDTH = ATT_HEADS * ATT_HEAD_DIM
Q_BLOCK = 128
HGRN_EXPAND = 128
HGRN_WIDTH = D_MODEL
HGRN_HEADS = HGRN_WIDTH // HGRN_EXPAND
HGRN_CHUNK = 64
X_HEADS = 4
X_HEAD_DIM = D_MODEL // X_HEADS
ROPE_THETA = 10000.0
IN_SIZES = (N_ATT_GROUPS * ATT_WIDTH,) * 3 + (HGRN_WIDTH,) * 4 + (D_MODEL,) * 2
N_IN = sum(IN_SIZES)


def rms_norm_2(x, g):
    xf = x.astype(jnp.float32)
    y = xf * lax.rsqrt(jnp.mean(xf * xf, axis=-1, keepdims=True) + EPS)
    return (y * g.astype(jnp.float32)).astype(x.dtype)

def swiglu_2(h, w_gu, w_down):
    gate, up = jnp.split(h @ w_gu, 2, axis=-1)
    return (jax.nn.silu(gate) * up) @ w_down

def rope_tables(positions, dim, dtype):
    inv_freq = ROPE_THETA ** (-jnp.arange(0, dim, 2, dtype=jnp.float32) / dim)
    ang = positions.astype(jnp.float32)[..., None] * inv_freq
    cos = jnp.cos(ang)[:, :, None, None, :].astype(dtype)
    sin = jnp.sin(ang)[:, :, None, None, :].astype(dtype)
    return cos, sin

def apply_rope(x, cos, sin):
    x1, x2 = jnp.split(x, 2, axis=-1)
    return jnp.concatenate([x1 * cos - x2 * sin, x2 * cos + x1 * sin], axis=-1)

def dilated_attention(q, k, v):
    B, T, G, H, dh = q.shape
    n_blk = T // Q_BLOCK
    scale = dh ** -0.5
    k_groups = [k[:, :, gi] for gi in range(G)]
    v_groups = [v[:, :, gi] for gi in range(G)]

    def block(b):
        t0 = b * Q_BLOCK
        tq = t0 + jnp.arange(Q_BLOCK)
        q_blk = lax.dynamic_slice_in_dim(q, t0, Q_BLOCK, axis=1)
        outs, lses = [], []
        for gi, (window, dil) in enumerate(ATT_GROUPS):
            j = jnp.arange(window // dil + 1)
            idx = tq[:, None] - dil * j[None, :]
            valid = idx >= 0
            idx = jnp.maximum(idx, 0)
            k_sel = k_groups[gi][:, idx]
            v_sel = v_groups[gi][:, idx]
            s = jnp.einsum('bqhd,bqjhd->bqhj', q_blk[:, :, gi], k_sel,
                           preferred_element_type=jnp.float32) * scale
            s = jnp.where(valid[None, :, None, :], s, -jnp.inf)
            m = jnp.max(s, axis=-1, keepdims=True)
            p = jnp.exp(s - m)
            den = jnp.sum(p, axis=-1)
            o = jnp.einsum('bqhj,bqjhd->bqhd', p, v_sel.astype(jnp.float32)) / den[..., None]
            outs.append(o)
            lses.append(m[..., 0] + jnp.log(den))
        w = jax.nn.softmax(jnp.stack(lses, axis=-1), axis=-1)
        o = jnp.einsum('bqhgd,bqhg->bqhd', jnp.stack(outs, axis=-2), w)
        return o.astype(q.dtype)

    o = lax.map(block, jnp.arange(n_blk))
    return o.transpose(1, 0, 2, 3, 4).reshape(B, T, H * dh)

def hgrn2_recurrence(q, f_logit, i, lb):
    B, T, H, N = q.shape
    C = HGRN_CHUNK
    NC = T // C
    lb = lb.reshape(H, N).astype(jnp.float32)
    f = lb + (1.0 - lb) * jax.nn.sigmoid(f_logit.astype(jnp.float32))
    g = jnp.log(f)
    k = 1.0 - f
    qs = q.astype(jnp.float32) * (N ** -0.5)

    def to_chunks(a):
        return a.reshape(B, NC, C, H, a.shape[-1]).transpose(1, 0, 3, 2, 4)

    causal = jnp.tril(jnp.ones((C, C), dtype=bool))

    def step(S, inp):
        qc, kc, vc, gc = inp
        b = jnp.cumsum(gc, axis=2)
        diff = b[:, :, :, None, :] - b[:, :, None, :, :]
        decay = jnp.exp(jnp.where(causal[:, :, None], diff, -jnp.inf))
        A = jnp.einsum('bhtn,bhsn,bhtsn->bhts', qc, kc, decay)
        o = (jnp.einsum('bhts,bhsv->bhtv', A, vc)
             + jnp.einsum('bhtn,bhnv->bhtv', qc * jnp.exp(b), S))
        b_last = b[:, :, -1:, :]
        S = (jnp.exp(b_last[:, :, 0, :])[..., None] * S
             + jnp.einsum('bhsn,bhsv->bhnv', kc * jnp.exp(b_last - b), vc))
        return S, o

    S0 = jnp.zeros((B, H, N, i.shape[-1]), jnp.float32)
    _, o = lax.scan(step, S0, (to_chunks(qs), to_chunks(k),
                               to_chunks(i.astype(jnp.float32)), to_chunks(g)))
    return o.transpose(1, 0, 3, 2, 4).reshape(B, T, H, -1)

def cross_attention(h, mem_n, wq, wkv, wo):
    B, T, _ = h.shape
    M = mem_n.shape[1]
    q = (h @ wq).reshape(B, T, X_HEADS, X_HEAD_DIM)
    k, v = jnp.split(mem_n @ wkv, 2, axis=-1)
    k = k.reshape(B, M, X_HEADS, X_HEAD_DIM)
    v = v.reshape(B, M, X_HEADS, X_HEAD_DIM)
    s = jnp.einsum('bthd,bmhd->bhtm', q, k, preferred_element_type=jnp.float32) * (X_HEAD_DIM ** -0.5)
    p = jax.nn.softmax(s, axis=-1)
    o = jnp.einsum('bhtm,bmhd->bthd', p, v.astype(jnp.float32)).astype(h.dtype)
    return o.reshape(B, T, X_HEADS * X_HEAD_DIM) @ wo

def second_inputs(seed: int = 0) -> dict:
    key = jax.random.key(seed)
    ks = iter(jax.random.split(key, 32))
    f32 = jnp.float32

    def w(shape, fan_in):
        return jax.random.normal(next(ks), shape, f32) * (fan_in ** -0.5)

    def gain(shape):
        return 1.0 + 0.02 * jax.random.normal(next(ks), shape, f32)

    L = DEPTH
    return {
        "x": jax.random.normal(next(ks), (BATCH, SEQ, D_MODEL), f32),
        "mem": jax.random.normal(next(ks), (BATCH, N_MEM, D_MODEL), f32),
        "positions": jnp.broadcast_to(jnp.arange(SEQ, dtype=jnp.int32), (BATCH, SEQ)),
        "ffn1_norm": gain((L, D_MODEL)),
        "ffn1_w_gu": w((L, D_MODEL, 2 * D_FF), D_MODEL),
        "ffn1_w_down": w((L, D_FF, D_MODEL), D_FF),
        "mix_norm": gain((L, D_MODEL)),
        "w_in": w((L, D_MODEL, N_IN), D_MODEL),
        "hgrn_lower_bounds": 0.1 * jax.random.normal(next(ks), (L, HGRN_WIDTH), f32),
        "hgrn_head_norm": gain((L, HGRN_WIDTH)),
        "w_att_branch": w((L, ATT_WIDTH, D_MODEL), ATT_WIDTH),
        "w_hgrn_branch": w((L, HGRN_WIDTH, D_MODEL), HGRN_WIDTH),
        "w_mix_out": w((L, D_MODEL, D_MODEL), D_MODEL),
        "xattn_norm": gain((L, D_MODEL)),
        "mem_norm": gain((L, D_MODEL)),
        "xattn_wq": w((L, D_MODEL, X_HEADS * X_HEAD_DIM), D_MODEL),
        "xattn_wkv": w((L, D_MODEL, 2 * X_HEADS * X_HEAD_DIM), D_MODEL),
        "xattn_wo": w((L, X_HEADS * X_HEAD_DIM, D_MODEL), X_HEADS * X_HEAD_DIM),
        "ffn2_norm": gain((L, D_MODEL)),
        "ffn2_w_gu": w((L, D_MODEL, 2 * D_FF), D_MODEL),
        "ffn2_w_down": w((L, D_FF, D_MODEL), D_FF),
        "final_norm": gain((D_MODEL,)),
    }

def second_block(x, mem, positions, ffn1_norm, ffn1_w_gu, ffn1_w_down, mix_norm, w_in,
              hgrn_lower_bounds, hgrn_head_norm, w_att_branch, w_hgrn_branch, w_mix_out,
              xattn_norm, mem_norm, xattn_wq, xattn_wkv, xattn_wo,
              ffn2_norm, ffn2_w_gu, ffn2_w_down, final_norm):
    B, T, _ = x.shape
    cos, sin = rope_tables(positions, ATT_HEAD_DIM, x.dtype)
    lb_p = jax.nn.softmax(hgrn_lower_bounds.astype(jnp.float32), axis=0)
    lb_all = jnp.cumsum(lb_p, axis=0) - lb_p[0]
    split_at = [sum(IN_SIZES[:n]) for n in range(1, len(IN_SIZES))]

    for l in range(DEPTH):
        x = x + 0.5 * swiglu_2(rms_norm_2(x, ffn1_norm[l]), ffn1_w_gu[l], ffn1_w_down[l])

        h = rms_norm_2(x, mix_norm[l])
        z = h @ w_in[l]
        q_a, k_a, v_a, q_b, f_b, i_b, og_b, gate_a, gate_b = jnp.split(z, split_at, axis=-1)
        att_shape = (B, T, N_ATT_GROUPS, ATT_HEADS, ATT_HEAD_DIM)
        q_a = apply_rope(q_a.reshape(att_shape), cos, sin)
        k_a = apply_rope(k_a.reshape(att_shape), cos, sin)
        v_a = v_a.reshape(att_shape)
        y_a = dilated_attention(q_a, k_a, v_a) @ w_att_branch[l]

        hg_shape = (B, T, HGRN_HEADS, HGRN_EXPAND)
        o_b = hgrn2_recurrence(q_b.reshape(hg_shape), f_b.reshape(hg_shape),
                               i_b.reshape(hg_shape), lb_all[l])
        o_b = rms_norm_2(o_b, hgrn_head_norm[l].reshape(HGRN_HEADS, HGRN_EXPAND))
        o_b = o_b.reshape(B, T, HGRN_WIDTH).astype(x.dtype) * jax.nn.silu(og_b)
        y_b = o_b @ w_hgrn_branch[l]

        merged = jax.nn.sigmoid(gate_a) * y_a + jax.nn.sigmoid(gate_b) * y_b
        x = x + merged @ w_mix_out[l]

        x = x + cross_attention(rms_norm_2(x, xattn_norm[l]), rms_norm_2(mem, mem_norm[l]),
                                xattn_wq[l], xattn_wkv[l], xattn_wo[l])

        x = x + 0.5 * swiglu_2(rms_norm_2(x, ffn2_norm[l]), ffn2_w_gu[l], ffn2_w_down[l])

    return rms_norm_2(x, final_norm)


def setup_inputs(seed=0):
    out = dict(first_inputs(seed))
    for name, value in second_inputs(seed + 1).items():
        if name != "x":
            out[name + "_2"] = value
    return out


def reference(
    x, ffn1_norm, ffn1_w_gate, ffn1_w_up, ffn1_w_down, mix_norm, w_in, gla_w_gate_up,
    gla_b_gate, gla_norm, fox_b_forget, fox_q_norm, fox_k_norm, fox_out_norm, ssm_conv_w,
    ssm_conv_b, ssm_dt_bias, ssm_A_log, ssm_D, ssm_norm, sc_conv_w, sc_out_norm, w_out,
    ffn2_norm, ffn2_w_gate, ffn2_w_up, ffn2_w_down, mem_2, positions_2, ffn1_norm_2,
    ffn1_w_gu_2, ffn1_w_down_2, mix_norm_2, w_in_2, hgrn_lower_bounds_2, hgrn_head_norm_2,
    w_att_branch_2, w_hgrn_branch_2, w_mix_out_2, xattn_norm_2, mem_norm_2, xattn_wq_2,
    xattn_wkv_2, xattn_wo_2, ffn2_norm_2, ffn2_w_gu_2, ffn2_w_down_2, final_norm_2,
):
    x = first_block(
        x, ffn1_norm, ffn1_w_gate, ffn1_w_up, ffn1_w_down, mix_norm, w_in, gla_w_gate_up,
        gla_b_gate, gla_norm, fox_b_forget, fox_q_norm, fox_k_norm, fox_out_norm, ssm_conv_w,
        ssm_conv_b, ssm_dt_bias, ssm_A_log, ssm_D, ssm_norm, sc_conv_w, sc_out_norm, w_out,
        ffn2_norm, ffn2_w_gate, ffn2_w_up, ffn2_w_down,
    )
    return second_block(
        x, mem_2, positions_2, ffn1_norm_2, ffn1_w_gu_2, ffn1_w_down_2, mix_norm_2, w_in_2,
        hgrn_lower_bounds_2, hgrn_head_norm_2, w_att_branch_2, w_hgrn_branch_2, w_mix_out_2,
        xattn_norm_2, mem_norm_2, xattn_wq_2, xattn_wkv_2, xattn_wo_2, ffn2_norm_2, ffn2_w_gu_2,
        ffn2_w_down_2, final_norm_2,
    )


_drawn_inputs = setup_inputs


def setup_inputs(seed=0):
    import zlib

    import numpy as np

    out = dict(_drawn_inputs(seed))
    spreads = {}
    factors = {'ffn1_norm': 2.892,
     'gla_b_gate': 3.411,
     'gla_norm': 7.067,
     'fox_q_norm': 5.343,
     'fox_k_norm': 6.597,
     'fox_out_norm': 4.093,
     'ssm_conv_b': 2.873,
     'ssm_norm': 4.406,
     'sc_out_norm': 4.464,
     'ffn2_norm': 5.26,
     'ffn1_norm_2': 7.552,
     'mix_norm_2': 4.664,
     'hgrn_lower_bounds_2': 3.732,
     'hgrn_head_norm_2': 8.0,
     'xattn_norm_2': 8.0,
     'mem_norm_2': 8.0,
     'ffn2_norm_2': 8.0,
     'final_norm_2': 2.833}
    for name, (base, spread) in spreads.items():
        noise = np.random.default_rng([zlib.crc32(name.encode()), seed]).standard_normal(out[name].shape)
        drawn = base * np.exp(spread * noise) if base else spread * noise
        out[name] = jnp.asarray(drawn.astype(out[name].dtype))
    for name, factor in factors.items():
        out[name] = (out[name] * factor).astype(out[name].dtype)
    return out
```

```python
from contextlib import ExitStack

import numpy as np

import concourse.bass as bass
from concourse import mybir

P = 128
T = 256
TT = T // P
D = 1024
KD = D // P
DFF = 2816
NF = DFF // T
DEPTH = 2
EPS = 1e-6
NEG = -1e30
RING = 6
CW = 256

ALU = mybir.AluOpType
ACT = mybir.ActivationFunctionType
AX = mybir.AxisListType.X
F32 = mybir.dt.float32
I32 = mybir.dt.int32

A_Q, A_K, A_V, A_G, A_LR = 0, 256, 512, 768, 1024
B_Q, B_K, B_V, B_F = 1040, 1296, 1552, 1808
C_Z, C_X, C_B, C_C, C_DT = 1812, 2068, 2324, 2580, 2836
D_B, D_C, D_V = 2840, 3096, 3352
PROJ1 = [("a_q", A_Q, "F"), ("a_k", A_K, "F"), ("a_v", A_V, "T"), ("xs", C_X, "F"), ("B", C_B, "F"),
         ("C", C_C, "F"), ("b_q", B_Q, "F"), ("b_k", B_K, "F"), ("b_v", B_V, "T"), ("d_c", D_C, "F"),
         ("d_v", D_V, "F"), ("d_b", D_B, "F"), ("a_g", A_G, "F"), ("c_z", C_Z, "F")]
AW = 3 * 512
H_Q, H_F, H_I, H_O = 3 * AW, 3 * AW + D, 3 * AW + 2 * D, 3 * AW + 3 * D
G_A, G_B = 3 * AW + 4 * D, 3 * AW + 5 * D
PROJ2 = ([("f", H_F + CW * c, "F", c) for c in range(4)] + [("q", H_Q + CW * c, "F", c) for c in range(4)]
         + [("i", H_I + CW * c, "T", c) for c in range(4)] + [("og", H_O + CW * c, "F", c) for c in range(4)]
         + [("aq", CW * c, "F", c) for c in range(6)] + [("ak", AW + CW * c, "F", c) for c in range(6)]
         + [("av", 2 * AW + CW * c, "T", c) for c in range(6)])
GATES = [("ga", G_A + CW * c, "F", c) for c in range(4)] + [("gb", G_B + CW * c, "F", c) for c in range(4)]

ROWS1 = [("ffn1_norm", 8), ("mix_norm", 8), ("ffn2_norm", 8), ("gla_b_gate", 2), ("gla_norm", 2),
         ("fox_out_norm", 2), ("ssm_conv_b", 6), ("ssm_norm", 2), ("sc_out_norm", 2),
         ("ssm_conv_w", 24), ("sc_conv_w", 6), ("fox_q_norm", 1), ("fox_k_norm", 1)]
ROWS2 = [("ffn1_norm_2", 8), ("mix_norm_2", 8), ("hgrn_head_norm_2", 8), ("xattn_norm_2", 8),
         ("mem_norm_2", 8), ("ffn2_norm_2", 8)]


def row_starts(rows):
    at, out = 0, {}
    for name, n in rows:
        out[name] = at
        at += n
    return out, at


COL1, NROW1 = row_starts(ROWS1)
COL2, NROW2 = row_starts(ROWS2)
LEVELS = [1, 2, 4, 8, 16, 32, 64, 128]


class Step:

    def __init__(self, eng, sem):
        self.eng, self.sem, self.n = eng, sem, 0

    def link(self, ins):
        ins.then_inc(self.sem, 1)
        self.n += 1

    def wait(self):
        if self.n:
            self.eng.wait_ge(self.sem, self.n)

    def then(self, ins):
        self.link(ins)
        self.wait()


def build(nc, A, out):
    with ExitStack() as ctx:
        def sb(name, shape, dt=F32):
            return ctx.enter_context(nc.sbuf_tensor(name, shape, dt))

        sems = {}
        scope = [ExitStack()]

        def S(name):
            if name not in sems:
                sems[name] = scope[0].enter_context(nc.semaphore(name))
            return sems[name]

        def clear_signals():
            with nc.Block() as block:
                @block.gpsimd
                def _(pool):
                    for s in sems.values():
                        pool.sem_clear(s)

        def end_part():
            scope[0].close()
            scope[0] = ExitStack()
            sems.clear()

        PS = ctx.enter_context(nc.psum_tensor("PS", [P, 8, 512], F32))

        xT = sb("xT", [P, KD, T])
        hT = sb("hT", [P, KD, T])
        ring = sb("ring", [P, RING, KD * CW])
        sq = sb("sq", [P, KD, T])
        rstd = sb("rstd", [P, T])
        ident = sb("ident", [P, P])
        ones = sb("ones", [P, P])
        ones64 = sb("ones64", [P, P])
        upper = sb("upper", [P, 3 * P])
        neg_causal = sb("neg_causal", [P, 2 * P])
        epst = sb("epst", [P, 1])
        prow = sb("prow", [P, P])
        pcol = sb("pcol", [P, P])
        work = sb("work", [P, 4096])
        g_sc, u_sc, s_sb, h_ff = (work[:, 1024 * i:1024 * (i + 1)].rearrange("p (b n) -> p b n", b=2)
                                  for i in range(4))
        soft_w, soft_t = (work[:, 1536 * i:1536 * (i + 1)].rearrange("p (b n) -> p b n", b=2) for i in range(2))
        soft_m = sb("soft_m", [P, 2, 4])
        zeros = sb("zeros", [P, P])
        ARENA = 28900
        arena = sb("arena", [P, ARENA])

        def carve():
            at = [0]

            def take(*shape, at_=None):
                n = int(np.prod(shape))
                a0 = at[0] if at_ is None else at_
                assert a0 + n <= ARENA, (a0, n)
                ap = arena[:, a0:a0 + n]
                if at_ is None:
                    at[0] += n
                if len(shape) == 1:
                    return ap
                names = "abcd"[:len(shape)]
                return ap.rearrange(f"p ({' '.join(names)}) -> p {' '.join(names)}",
                                    **{c: s for c, s in zip(names, shape)})
            take.at = at
            return take

        def bank(b, n=512):
            return PS[:, b, 0:n]

        def bank2(b):
            return PS[:, b, :].rearrange("p (a n) -> p a n", a=2)

        def over(ap, k):
            return ap.unsqueeze(1).broadcast_to([P, k, ap.shape[-1]])


        def load_chunk(sp, n, src, dst_shape, i=0):
            sp.wait_ge(S("chunk_done"), n + 1 + i * RING)
            k, w = dst_shape
            dst = ring[:, n % RING, 0:k * w].rearrange("p (k w) -> p k w", k=k)
            sp.dma_start(dst, src).then_inc(S(f"landed{n % RING}"), 16)

        def chunk(n, k, w):
            return ring[:, n % RING, 0:k * w].rearrange("p (k w) -> p k w", k=k)

        def wait_chunk(pe, n, i=0):
            pe.wait_ge(S(f"landed{n % RING}"), 16 * (n // RING + 1) + i * 16)

        def norm_act(act, p, src, ready=None):
            for j in range(4):
                if ready:
                    act.wait_ge(ready, j + 1)
                act.activation(sq[:, 2 * j:2 * j + 2, :], src[:, 2 * j:2 * j + 2, :], ACT.Square)\
                   .then_inc(S(p + "squares"), 1)
            act.wait_ge(S(p + "sums"), 1)
            act.activation(rstd[:], bank(4, T), ACT.Sqrt, scale=1.0 / D, bias=epst[:, 0:1])\
               .then_inc(S(p + "root"), 1)

        def norm_pe(pe, p):
            for k in range(KD):
                if k % 2 == 0:
                    pe.wait_ge(S(p + "squares"), k // 2 + 1)
                m = pe.matmul(bank(4, T), ones[:], sq[:, k, :], start=(k == 0), stop=(k == KD - 1))
            m.then_inc(S(p + "sums"), 1)

        def norm_dve(dve, p):
            dve.wait_ge(S(p + "root"), 1)
            dve.reciprocal(rstd[:], rstd[:]).then_inc(S(p + "rstd"), 1)
            dve.wait_ge(S(p + "rstd"), 1)

        def scaled_dve(dve, p, dst, src, gain, with_rstd, ready=None):
            for k in range(KD):
                if ready and k % 2 == 0:
                    dve.wait_ge(ready, k // 2 + 1)
                if with_rstd:
                    dve.scalar_tensor_tensor(dst[:, k, :], src[:, k, :], pcol[:, gain + k:gain + k + 1], rstd[:],
                                             ALU.mult, ALU.mult).then_inc(S(p + "in_ready"), 1)
                else:
                    dve.tensor_scalar(dst[:, k, :], src[:, k, :], pcol[:, gain + k:gain + k + 1], None,
                                      ALU.mult).then_inc(S(p + "in_ready"), 1)

        def ffn_sp(sp, c0, wg, wu, wd):
            def cols(w, s):
                return w[:, bass.ts(s, CW)].rearrange("(k p) f -> p k f", p=P)

            def rows(s):
                return wd[bass.ts(s, T), :].rearrange("(k p) f -> p k f", p=P)
            load_chunk(sp, c0, cols(wg, 0), (KD, CW))
            load_chunk(sp, c0 + 1, cols(wu, 0), (KD, CW))
            with sp.Fori(0, (NF - 1) // 2) as i:
                for j in range(2):
                    s = 2 * i + (1 + j)
                    n = c0 + 2 + 3 * j
                    load_chunk(sp, n, cols(wg, s), (KD, CW), i)
                    load_chunk(sp, n + 1, cols(wu, s), (KD, CW), i)
                    load_chunk(sp, n + 2, rows(s - 1), (2, D), i)
            load_chunk(sp, c0 + 3 * NF - 1, rows(NF - 1), (2, D))

        def ffn_pe(pe, p, c0):
            def up(n, b, i=0, first=False):
                w = chunk(n, KD, CW)
                wait_chunk(pe, n, i)
                for f in range(2):
                    for k in range(KD):
                        if first and f == 0:
                            pe.wait_ge(S(p + "in_ready"), k + 1)
                        m = pe.matmul(bank2(b)[:, f, :], w[:, k, f * P:(f + 1) * P], hT[:, k, :],
                                      start=(k == 0), stop=(k == KD - 1))
                m.then_inc(S("chunk_done"), 1)

            def down(n, b, i, hs, last):
                w = chunk(n, 2, D)
                wait_chunk(pe, n, i)
                pe.wait_ge(S(p + "hidden"), hs)
                for k in range(2):
                    for o in range(KD):
                        m = pe.matmul(bank2(4 + o // 2)[:, o % 2, :], w[:, k, o * P:(o + 1) * P],
                                      h_ff[:, b, k * T:(k + 1) * T],
                                      start=False, stop=(last and k == 1),
                                      skip_group_check=True)
                m.then_inc(S("chunk_done"), 1)

            up(c0, 0, first=True)
            up(c0 + 1, 2)
            norm_pe(pe, p)
            zero_sums_pe(pe, p)
            with pe.Fori(0, (NF - 1) // 2) as i:
                for j in range(2):
                    n = c0 + 2 + 3 * j
                    up(n, 1 - j, i)
                    up(n + 1, 3 - j, i)
                    down(n + 2, j, i, 2 * i + (1 + j), False)
            down(c0 + 3 * NF - 1, 0, 0, NF, True)

        def zero_sums_pe(pe, p):
            pe.wait_ge(S(p + "root"), 1)
            for b in range(4, 8):
                pe.matmul(bank(b, 2), zeros[:], zeros[:, 0:2], start=True, stop=False, skip_group_check=True)

        def ffn_act(act, p, c0):
            def silu(b, n_gs):
                act.wait_ge(S(p + "gate_scaled"), n_gs)
                act.activation(s_sb[:, b, :], g_sc[:, b, :], ACT.Silu).then_inc(S(p + "silu"), 1)
            silu(0, 1)
            with act.Fori(0, (NF - 1) // 2) as i:
                for j in range(2):
                    silu(1 - j, 2 * i + (2 + j))

        def ffn_dve(dve, p, c0):
            def step(b, s, n_done, n_prev_down):
                dve.wait_ge(S("chunk_done"), n_done)
                dve.tensor_tensor(g_sc[:, b, :].rearrange("p (a n) -> p a n", a=2), bank2(b), over(rstd[:], 2),
                                  ALU.mult).then_inc(S(p + "gate_scaled"), 1)
                dve.wait_ge(S("chunk_done"), n_done + 1)
                dve.tensor_tensor(u_sc[:, b, :].rearrange("p (a n) -> p a n", a=2), bank2(2 + b), over(rstd[:], 2),
                                  ALU.mult).then_inc(S(p + "up_scaled"), 1)
                dve.wait_ge(S(p + "up_scaled"), s + 1)
                dve.wait_ge(S(p + "silu"), s + 1)
                if n_prev_down is not None:
                    dve.wait_ge(S("chunk_done"), n_prev_down)
                dve.tensor_tensor(h_ff[:, b, :], s_sb[:, b, :], u_sc[:, b, :], ALU.mult)\
                   .then_inc(S(p + "hidden"), 1)
            step(0, 0, RING + c0 + 1, None)
            with dve.Fori(0, (NF - 1) // 2) as i:
                for j in range(2):
                    n = c0 + 2 + 3 * j
                    step(1 - j, 2 * i + (1 + j), i * RING + (RING + n + 1), i * RING + (RING + n))
            dve.wait_ge(S("chunk_done"), RING + c0 + 3 * NF)
            for j in range(4):
                x2 = xT[:, 2 * j:2 * j + 2, :]
                dve.scalar_tensor_tensor(x2, bank2(4 + j), 0.5, x2, ALU.mult, ALU.add)\
                   .then_inc(S(p + "x_ready"), 1)

        def gemm_sp(sp, c0, srcs, k=KD):
            for n, src in enumerate(srcs):
                load_chunk(sp, c0 + n, src, (k, CW))

        def gemm_pe(pe, c0, layouts, rhs, evac, ev0=0, k_=KD, ready=None, first_n=0):
            for n, lay in enumerate(layouts):
                w = chunk(c0 + n, k_, CW)
                b = n % 4
                wait_chunk(pe, c0 + n)
                if n >= 4:
                    pe.wait_ge(S(evac), ev0 + n - 3)
                for f in range(2):
                    for k in range(k_):
                        if ready and n == 0 and f == 0:
                            pe.wait_ge(ready, k + 1)
                        if lay == "F":
                            m = pe.matmul(bank2(b)[:, f, :], w[:, k, f * P:(f + 1) * P], rhs[:, k, :],
                                          start=(k == 0), stop=(k == k_ - 1))
                        else:
                            m = pe.matmul(bank2(b)[:, f, :], rhs[:, k, f * P:(f + 1) * P], w[:, k, :],
                                          start=(k == 0), stop=(k == k_ - 1))
                m.then_inc(S("chunk_done"), 1)

        def gemm_pe1(pe, n, b, rhs, lay="F"):
            w = chunk(n, KD, CW)
            wait_chunk(pe, n)
            for f in range(2):
                for k in range(KD):
                    a, r = ((w[:, k, f * P:(f + 1) * P], rhs[:, k, :]) if lay == "F" else
                            (rhs[:, k, f * P:(f + 1) * P], w[:, k, :]))
                    m = pe.matmul(bank2(b)[:, f, :], a, r, start=(k == 0), stop=(k == KD - 1))
            m.then_inc(S("chunk_done"), 1)

        def residual_dve(dve, p, c0):
            for n in range(4):
                dve.wait_ge(S("chunk_done"), RING + c0 + n + 1)
                x2 = xT[:, 2 * n:2 * n + 2, :]
                dve.tensor_tensor(x2, bank2(n), x2, ALU.add).then_inc(S(p + "x_ready"), 1)

        def colchunks(w, offs, kt=KD):
            return [w[:, o:o + CW].rearrange("(k p) f -> p k f", p=P) for o in offs]

        class Soft:
            def __init__(self, p, units, wide, scale):
                self.p, self.units, self.scale, self.wide = p, units, scale, wide

            def area(self, u, n):
                a = PS[:, 4 + 2 * (u % 2):6 + 2 * (u % 2), :].rearrange("p a n -> p (a n)")
                return a[:, 0:n]

        def soft_pe(pe, sf, ev_bank):
            U = len(sf.units)
            p = sf.p
            for u in range(U + 2):
                if u < U:
                    if u >= 2:
                        pe.wait_ge(S(p + "max"), u - 1)
                        pe.wait_ge(S(p + "exp"), u - 1)
                    m = sf.units[u]["score"](pe, sf.area(u, sf.units[u]["n"]))
                    m.then_inc(S(p + "scores"), 1)
                if 1 <= u <= U:
                    v = u - 1
                    pe.wait_ge(S(p + "weights"), v + 1)
                    if v >= 1:
                        pe.wait_ge(S(p + "turned"), v)
                    for t in range(sf.units[v]["n"] // P):
                        m = pe.transpose(PS[:, t // 4, (t % 4) * P:(t % 4 + 1) * P],
                                         soft_w[:, v % 2, t * P:(t + 1) * P], ident[:])
                    m.then_inc(S(p + "turn"), 1)
                if u >= 2:
                    v = u - 2
                    pe.wait_ge(S(p + "turned"), v + 1)
                    w = ev_bank(v)
                    if w:
                        pe.wait_ge(S(p + "o_out"), w)
                    m = sf.units[v]["pv"](pe, soft_t[:, v % 2, :])
                    m.then_inc(S(p + "pv"), 1)

        def soft_dve(dve, st, sf):
            U = len(sf.units)
            p = sf.p
            for u in range(U + 1):
                if u < U:
                    n, mask = sf.units[u]["n"], sf.units[u]["mask"]
                    dve.wait_ge(S(p + "scores"), u + 1)
                    if u >= 2:
                        dve.wait_ge(S(p + "turn"), u - 1)
                    if mask is None:
                        st.then(dve.tensor_reduce(soft_m[:, u % 2, 0:1], sf.area(u, n), AX, ALU.max))
                    else:
                        st.then(dve.tensor_tensor_reduce(soft_w[:, u % 2, 0:n], sf.area(u, n), mask, 1.0, -3e38,
                                                         ALU.add, ALU.max, soft_m[:, u % 2, 0:1]))
                    dve.tensor_scalar(soft_m[:, u % 2, 1:2], soft_m[:, u % 2, 0:1], -sf.scale, None, ALU.mult)\
                       .then_inc(S(p + "max"), 1)
                if u >= 1:
                    v = u - 1
                    n = sf.units[v]["n"]
                    dve.wait_ge(S(p + "exp"), v + 1)
                    st.then(dve.reciprocal(soft_m[:, v % 2, 3:4], soft_m[:, v % 2, 2:3]))
                    dve.tensor_scalar(soft_w[:, v % 2, 0:n], soft_w[:, v % 2, 0:n], soft_m[:, v % 2, 3:4], None,
                                      ALU.mult).then_inc(S(p + "weights"), 1)

        def soft_act(act, sf, evacs):
            U = len(sf.units)
            p = sf.p
            for u in range(U + 2):
                if u < U:
                    n, mask = sf.units[u]["n"], sf.units[u]["mask"]
                    act.wait_ge(S(p + "max"), u + 1)
                    src = sf.area(u, n) if mask is None else soft_w[:, u % 2, 0:n]
                    act.activation(soft_w[:, u % 2, 0:n], src, ACT.Exp, scale=sf.scale, bias=soft_m[:, u % 2, 1:2],
                                   accum_out=soft_m[:, u % 2, 2:3]).then_inc(S(p + "exp"), 1)
                if 1 <= u <= U:
                    v = u - 1
                    n = sf.units[v]["n"]
                    act.wait_ge(S(p + "turn"), v + 1)
                    if v >= 2:
                        act.wait_ge(S(p + "pv"), v - 1)
                    act.activation(soft_t[:, v % 2, 0:n], PS[:, 0:2, :].rearrange("p a n -> p (a n)")[:, 0:n],
                                   ACT.Copy).then_inc(S(p + "turned"), 1)
                if u >= 2 and (u - 2) in evacs:
                    act.wait_ge(S(p + "pv"), u - 1)
                    dst, src = evacs[u - 2]
                    act.activation(dst, src, ACT.Copy).then_inc(S(p + "o_out"), 1)

        def ffn_pe_all(pe, p, c0):
            ffn_pe(pe, p, c0)

        def ffn_act_all(act, p, c0, ready):
            norm_act(act, p, xT, ready)
            ffn_act(act, p, c0)

        def ffn_dve_all(dve, p, c0, gain, ready):
            scaled_dve(dve, p, hT, xT, gain, False, ready)
            norm_dve(dve, p)
            ffn_dve(dve, p, c0)

        def halves(ap, m):
            v = ap.rearrange("p a t -> p (a t)").rearrange("p (b h m) -> p b h m", h=2, m=m)
            return v[:, :, 0, :], v[:, :, 1, :]

        def last_of(first, m):
            return first[:, :, m - 1:m].broadcast_to([P, first.shape[1], m])

        def apply_scores(pe, b, h, v, a):
            po, ct = 64 * (h % 2), h // 2
            o = bank2(b)[po:po + 64, ct, :]
            pe.matmul(o, v[:, 0, 64 * h:64 * h + 64], a[:, 0:T], start=True, stop=False, skip_group_check=True)
            return pe.matmul(o[:, P:T], v[:, 1, 64 * h:64 * h + 64], a[:, T:T + P], start=False, stop=True,
                             skip_group_check=True)

        def head_norm(dve, st, root, src, gain, tile, gate):
            dve.wait_ge(S(root), 1)
            st.then(dve.reciprocal(ors, ors))
            for c in range(2):
                m = dve.scalar_tensor_tensor(mix[:, tile + c, :], src[:, c, :], pcol[:, gain + c:gain + c + 1],
                                             ors[:, c, :], ALU.mult, ALU.mult)
                if gate is not None:
                    st.then(m)
                    m = dve.tensor_tensor(mix[:, tile + c, :], mix[:, tile + c, :], gate[:, c, :], ALU.mult)
            m.then_inc(S("mix_done"), 1)

        with nc.Block() as block:
            xin = hT[:].rearrange("p k t -> p (k t)").rearrange("p (a n) -> p a n", a=TT)

            @block.sync
            def _(sp):
                sp.dma_start(xin, A["x"][0].rearrange("(a p) n -> p a n", p=P)).then_inc(S("x_in"), 16)

            @block.gpsimd
            def _(pool):
                st = Step(pool, S("pool_step"))
                for m, v in ((ident, 0.0), (ones64, 0.0), (upper, 1.0), (neg_causal, 0.0), (ones, 1.0),
                             (zeros, 0.0), (epst, EPS)):
                    st.then(pool.memset(m[:], v))
                for c in range(2):
                    st.then(pool.memset(ones64[64 * c:64 * c + 64, 64 * c:64 * c + 64], 1.0))
                for c in (0, 2):
                    u = upper[:, c * P:(c + 1) * P]
                    st.then(pool.affine_select(out=u, in_=u, compare_op=ALU.is_ge, fill=0.0, base=0,
                                               pattern=[[1, P]], channel_multiplier=-1))
                u = neg_causal[:, P:2 * P]
                st.then(pool.affine_select(out=u, in_=u, compare_op=ALU.is_ge, fill=NEG, base=0, pattern=[[-1, P]],
                                           channel_multiplier=1))
                pool.affine_select(out=ident[:], in_=ident[:], compare_op=ALU.not_equal, fill=1.0, base=0,
                                   pattern=[[-1, P]], channel_multiplier=1).then_inc(S("masks"), 1)

            @block.tensor
            def _(pe):
                pe.wait_ge(S("masks"), 1)
                pe.wait_ge(S("x_in"), 16)
                for k in range(KD):
                    for a in range(TT):
                        m = pe.transpose(bank2(k // 2)[:, k % 2, a * P:(a + 1) * P], xin[:, a, k * P:(k + 1) * P],
                                         ident[:])
                    m.then_inc(S("x_turn"), 1)

            @block.vector
            def _(dve):
                for j in range(4):
                    dve.wait_ge(S("x_turn"), 2 * j + 2)
                    dve.tensor_copy(xT[:, 2 * j:2 * j + 2, :], bank2(j)).then_inc(S("x_out"), 1)

        clear_signals()
        end_part()

        take = carve()
        gq, gk, gg, fq, fk, sz, db, dc, dv = (take(2, T) for _ in range(9))
        gv, fv = take(2, T), take(2, T)
        PAD = 4
        xp, Bp, Cp, cp = (take(2, PAD + T) for _ in range(4))
        xs, Bc, Cc, cc = (take(2, T) for _ in range(4))
        mix = take(KD, T)
        wsm = take(KD, 24)
        wgu = take(T)
        lr = take(T)
        zg, za = take(2, T), take(2, T)
        Ef, Eg = take(2, T), take(2, T)
        Kd, Qd = take(2, T), take(2, T)
        K64 = take(2, 2, 64)
        K128, Q128 = take(2, P), take(2, P)
        tb = take(2, 8)
        tA, tD = take(4), take(4)
        dcol = take(2)
        tz, te, ta = take(2, 8), take(2, 8), take(2, 8)
        acs = take(2, 4)
        bcs = take(2, 8, P)
        at_ = take(2, 3 * P)
        Gm = take(2, 3 * P)
        Lm = take(2, 3 * P)
        xd = take(2, T)
        osb, osq, ors = take(2, T), take(2, T), take(2, T)
        with nc.Fori(0, DEPTH) as layer:
            W = {n: A[n][layer] for n in ("ffn1_w_gate", "ffn1_w_up", "ffn1_w_down", "ffn2_w_gate", "ffn2_w_up",
                                          "ffn2_w_down", "w_in", "w_out", "gla_w_gate_up")}
            c_ffn1, c_proj = 0, 3 * NF
            c_out = c_proj + len(PROJ1)
            c_ffn2 = c_out + 4
            fox_units = []
            for h in range(4):
                for t in range(2):
                    po, ct = 64 * (h % 2), h // 2

                    def score(pe, a, h=h, t=t, po=po, ct=ct):
                        n = P * (t + 1)
                        pe.matmul(a[:, 0:n], fq[po:po + 64, ct, t * P:(t + 1) * P], fk[po:po + 64, ct, 0:n],
                                  start=True, stop=False, skip_group_check=True)
                        m = pe.matmul(a[:, 0:n], bcs[:, 0, h, :], upper[:, 0:n], start=False, stop=(t == 0),
                                      skip_group_check=True)
                        if t == 1:
                            m = pe.matmul(a[:, P:2 * P], bcs[:, 1, h, :], upper[:, 0:P], start=False, stop=True,
                                          skip_group_check=True)
                        return m

                    def pv(pe, w, h=h, t=t, po=po, ct=ct):
                        o = bank2(2)[po:po + 64, ct, t * P:(t + 1) * P]
                        for j in range(t + 1):
                            m = pe.matmul(o, fv[:, j, 64 * h:64 * h + 64], w[:, j * P:(j + 1) * P],
                                          start=(j == 0), stop=(j == t), skip_group_check=True)
                        return m
                    fox_units.append({"n": P * (t + 1), "mask": neg_causal[:, P * (1 - t):2 * P],
                                      "score": score, "pv": pv})
            fox = Soft("fox_", fox_units, 2, 1.0)

            with nc.Block() as block:
                @block.sync
                def _(sp):
                    for name, n in ROWS1:
                        r0 = COL1[name]
                        src = A[name][layer]
                        if name in ("fox_q_norm", "fox_k_norm"):
                            for c in range(2):
                                sp.dma_start(prow[r0:r0 + 1, 64 * c:64 * c + 64],
                                             src.rearrange("(a n) -> a n", a=1)).then_inc(S("rows"), 16)
                        elif name.endswith("conv_w"):
                            sp.dma_start(prow[r0:r0 + n, :], src.rearrange("j (k p) -> (j k) p", p=P))\
                              .then_inc(S("rows"), 16)
                        else:
                            sp.dma_start(prow[r0:r0 + n, :], src.rearrange("(k p) -> k p", p=P))\
                              .then_inc(S("rows"), 16)
                    ffn_sp(sp, c_ffn1, W["ffn1_w_gate"], W["ffn1_w_up"], W["ffn1_w_down"])
                    gemm_sp(sp, c_proj, colchunks(W["w_in"], [o for _, o, _ in PROJ1]))
                    gemm_sp(sp, c_out, colchunks(W["w_out"], [CW * c for c in range(4)]))
                    ffn_sp(sp, c_ffn2, W["ffn2_w_gate"], W["ffn2_w_up"], W["ffn2_w_down"])

                @block.gpsimd
                def _(pool):
                    pool.memset(at_, 0.0).then_inc(S("pool_zero"), 1)
                    for a in (xp, Bp, Cp, cp):
                        pool.memset(a[:, :, 0:PAD], 0.0).then_inc(S("pool_zero"), 1)

                @block.tensor
                def _(pe):
                    pe.sem_inc(S("chunk_done"), RING)
                    pe.wait_ge(S("rows"), 16 * (len(ROWS1) + 2))
                    pe.transpose(bank(0, NROW1), prow[0:NROW1, :], ident[0:NROW1, 0:NROW1])\
                      .then_inc(S("cols_turn"), 1)
                    pe.wait_ge(S("cols"), 1)
                    ffn_pe_all(pe, "ffn1_", c_ffn1)
                    norm_pe(pe, "mix_")
                    pe.wait_ge(S("small"), 16 * 10)
                    for k in range(KD):
                        pe.wait_ge(S("mix_in_ready"), k + 1)
                        m = pe.matmul(PS[0:16, 5, 0:T], wsm[:, k, 0:16], hT[:, k, :], start=(k == 0),
                                      stop=(k == KD - 1))
                    m.then_inc(S("lr_psum"), 1)
                    for t in range(2):
                        for k in range(KD):
                            m = pe.matmul(PS[:, 6, 8 * t:8 * t + 8], hT[:, k, t * P:(t + 1) * P], wsm[:, k, 16:24],
                                          start=(k == 0), stop=(k == KD - 1))
                    m.then_inc(S("tok_psum"), 1)
                    gemm_pe(pe, c_proj, [l for _, _, l in PROJ1], hT, "proj_out")
                    pe.wait_ge(S("lr"), 1)
                    for c in range(2):
                        m = pe.matmul(bank2(7)[:, c, :], wgu[0:16, c * P:(c + 1) * P], lr[0:16, :], start=True,
                                      stop=True)
                    m.then_inc(S("gate_psum"), 1)
                    pe.wait_ge(S("tok_vals"), 1)
                    pe.matmul(PS[:, 6, 32:36], upper[:, 0:P], ta[:, 0, 4:8], start=True, stop=True)
                    pe.matmul(PS[:, 6, 36:40], ones[:], ta[:, 0, 4:8], start=True, stop=False)
                    pe.matmul(PS[:, 6, 36:40], upper[:, 0:P], ta[:, 1, 4:8], start=False, stop=True)\
                      .then_inc(S("acs_psum"), 1)
                    pe.wait_ge(S("conv_out"), 6)
                    for c in range(2):
                        for t in range(2):
                            m = pe.transpose(bank2(0)[:, t, c * P:(c + 1) * P], xs[:, c, t * P:(t + 1) * P], ident[:])
                    m.then_inc(S("xs_turn"), 1)
                    for g in range(2):
                        pe.matmul(PS[:, 1 + g, 0:T], Bc[:, g, 0:P], Cc[:, g, :], start=True, stop=True)
                        m = pe.matmul(PS[:, 1 + g, T:T + P], Bc[:, g, P:T], Cc[:, g, P:T], start=True, stop=True)
                        m.then_inc(S("cb_psum"), 1)
                    pe.wait_ge(S("bcs"), 16)
                    pe.wait_ge(S("cb_masked"), 2)
                    pe.wait_ge(S("xd"), 1)
                    for h in range(5):
                        if h < 4:
                            if h >= 2:
                                pe.wait_ge(S("seg"), h - 1)
                            b = 4 + h % 2
                            pe.matmul(PS[:, b, 0:T], bcs[:, 0, 4 + h, :], upper[:, 0:T], start=True, stop=False,
                                      skip_group_check=True)
                            pe.matmul(PS[:, b, P:T], bcs[:, 1, 4 + h, :], upper[:, 0:P], start=False, stop=True,
                                      skip_group_check=True).then_inc(S("acs_row"), 1)
                        if h >= 1:
                            g = h - 1
                            pe.wait_ge(S("ssd_w"), g + 1)
                            m = apply_scores(pe, 3, g, xd, Lm[:, g % 2, :])
                            m.then_inc(S("ssd_pv"), 1)
                    pe.wait_ge(S("ssd_sq"), 1)
                    pe.matmul(bank(6), ones[:], osq, start=True, stop=True).then_inc(S("ssd_sum"), 1)
                    pe.wait_ge(S("sc_sq"), 1)
                    pe.matmul(bank(5), ones64[:], osq, start=True, stop=True).then_inc(S("sc_sum"), 1)
                    pe.wait_ge(S("gla_ops"), 1)
                    for h in range(5):
                        if h < 4:
                            po, ct = 64 * (h % 2), h // 2
                            b = 4 + h % 2
                            if h >= 2:
                                pe.wait_ge(S("gla_w"), h - 1)
                            hp = slice(po, po + 64)
                            for t in range(2):
                                o = t * P
                                c = 2 * t * P
                                pe.matmul(PS[0:64, b, c:c + 64], Kd[hp, ct, o:o + 64], Qd[hp, ct, o:o + 64],
                                          start=True, stop=True, skip_group_check=True)
                                pe.matmul(PS[0:64, b, c + 64:c + P], K64[hp, ct, t, :],
                                          Qd[hp, ct, o + 64:o + P], start=True, stop=True, skip_group_check=True)
                                pe.matmul(PS[64:128, b, c + 64:c + P], Kd[hp, ct, o + 64:o + P],
                                          Qd[hp, ct, o + 64:o + P], start=True, stop=True, skip_group_check=True)
                            pe.matmul(PS[:, b, P:2 * P], K128[hp, ct, :], Q128[hp, ct, :], start=True, stop=True,
                                      skip_group_check=True).then_inc(S("gla_maps"), 1)
                        if h >= 1:
                            g = h - 1
                            pe.wait_ge(S("gla_w"), g + 1)
                            m = apply_scores(pe, 3, g, gv, at_[:, g % 2, :])
                            m.then_inc(S("gla_pv"), 1)
                    pe.wait_ge(S("gla_sq"), 1)
                    pe.matmul(bank(6), ones64[:], osq, start=True, stop=True).then_inc(S("gla_sum"), 1)
                    pe.wait_ge(S("fox_qk_sq"), 2)
                    for c in range(2):
                        pe.matmul(bank(4 + c), ones64[:], (Ef, Eg)[c], start=True, stop=True)\
                          .then_inc(S("fox_qk_sum"), 1)
                    pe.wait_ge(S("fox_qk"), 2)
                    soft_pe(pe, fox, lambda v: 0)
                    pe.wait_ge(S("fox_sq"), 1)
                    pe.matmul(bank(6), ones64[:], osq, start=True, stop=True).then_inc(S("fox_sum"), 1)
                    pe.wait_ge(S("mix_done"), 4)
                    gemm_pe(pe, c_out, "FFFF", mix, "none")
                    ffn_pe_all(pe, "ffn2_", c_ffn2)

                @block.scalar
                def _(act):
                    st = Step(act, S("act_step"))
                    for o, n, at in ((A_LR, 16, 0), (B_F, 4, 16), (C_DT, 4, 20)):
                        act.dma_start(wsm[:, :, at:at + n], W["w_in"][:, o:o + n]
                                       .rearrange("(k p) f -> p k f", p=P)).then_inc(S("small"), 16)
                    act.dma_start(wgu[0:16, :], W["gla_w_gate_up"]).then_inc(S("small"), 16)
                    for t in range(2):
                        for name, at in (("fox_b_forget", 0), ("ssm_dt_bias", 4)):
                            act.dma_start(tb[:, t, at:at + 4], A[name][layer].partition_broadcast(P))\
                                .then_inc(S("small"), 16)
                    act.dma_start(tD, A["ssm_D"][layer].partition_broadcast(P)).then_inc(S("small"), 16)
                    act.dma_start(tA, A["ssm_A_log"][layer].partition_broadcast(P)).then_inc(S("small"), 16)
                    ffn_act_all(act, "ffn1_", c_ffn1, None)
                    norm_act(act, "mix_", xT, S("ffn1_x_ready"))
                    act.wait_ge(S("lr_psum"), 1)
                    act.activation(lr[0:16, :], PS[0:16, 5, 0:T], ACT.Copy).then_inc(S("lr"), 1)
                    pads = {"xs": xp, "B": Bp, "C": Cp}
                    dst = {"a_q": gq, "a_k": gk, "a_v": gv, "b_q": fq, "b_k": fk, "b_v": fv, "d_c": dc, "d_v": dv,
                           "d_b": db, "a_g": gg, "c_z": sz}
                    act.wait_ge(S("pool_zero"), 5)
                    for n, (name, _, lay) in enumerate(PROJ1):
                        act.wait_ge(S("chunk_done"), RING + c_proj + n + 1)
                        o = pads[name][:, :, PAD:PAD + T] if name in pads else dst[name]
                        f = ACT.Silu if name in ("a_g", "c_z") else ACT.Copy
                        act.activation(o, bank2(n % 4), f, scale=(0.125 if name == "a_q" else 1.0))\
                           .then_inc(S("proj_out"), 1)
                    for c in range(6):
                        act.wait_ge(S("conv_acc"), c + 1)
                        a = (xs, Bc, Cc)[c // 2][:, c % 2, :]
                        act.activation(a, a, ACT.Silu, bias=pcol[:, COL1["ssm_conv_b"] + c:COL1["ssm_conv_b"] + c + 1])\
                           .then_inc(S("conv_out"), 1)
                    act.wait_ge(S("gate_psum"), 1)
                    for c in range(2):
                        g = act.activation(zg[:, c, :], bank2(7)[:, c, :], ACT.Identity,
                                           bias=pcol[:, COL1["gla_b_gate"] + c:COL1["gla_b_gate"] + c + 1])
                    g.then_inc(S("gate_z"), 1)
                    act.wait_ge(S("gate_z"), 1)
                    st.then(act.activation(Ef, zg, ACT.Abs))
                    st.then(act.activation(Ef, Ef, ACT.Exp, scale=-1.0))
                    act.activation(Ef, Ef, ACT.Ln, bias=1.0).then_inc(S("gate_ln"), 1)
                    act.wait_ge(S("tok_z"), 1)
                    st.then(act.activation(te, tz, ACT.Abs))
                    st.then(act.activation(te, te, ACT.Exp, scale=-1.0))
                    act.activation(te, te, ACT.Ln, bias=1.0).then_inc(S("tok_ln"), 1)
                    act.wait_ge(S("small"), 16 * 10)
                    act.activation(tA, tA, ACT.Exp).then_inc(S("A_exp"), 1)
                    act.wait_ge(S("gla_pref"), 1)
                    act.activation(Ef, za, ACT.Exp)
                    act.activation(Eg, za, ACT.Exp, scale=-1.0)
                    act.activation(K64, K64, ACT.Exp).then_inc(S("gla_exp"), 1)
                    act.wait_ge(S("gla_pref"), 2)
                    act.activation(Q128, za[:, :, P:T], ACT.Exp)
                    act.activation(K128, K128, ACT.Exp).then_inc(S("gla_exp"), 1)
                    for h in range(4):
                        act.wait_ge(S("seg"), h + 1)
                        act.activation(Lm[:, h % 2, :], Lm[:, h % 2, :], ACT.Exp).then_inc(S("seg_exp"), 1)
                    act.wait_ge(S("ssd_y"), 1)
                    act.activation(osq, osb, ACT.Square).then_inc(S("ssd_sq"), 1)
                    act.wait_ge(S("ssd_sum"), 1)
                    act.activation(ors, bank2(6), ACT.Sqrt, scale=1.0 / P, bias=epst[:, 0:1]).then_inc(S("ssd_root"), 1)
                    act.wait_ge(S("sc_y"), 1)
                    act.activation(osq, db, ACT.Square).then_inc(S("sc_sq"), 1)
                    act.wait_ge(S("sc_sum"), 1)
                    act.wait_ge(S("mix_done"), 1)
                    act.activation(ors, bank2(5), ACT.Sqrt, scale=1.0 / 64, bias=epst[:, 0:1])\
                       .then_inc(S("sc_root"), 1)
                    for h in range(4):
                        act.wait_ge(S("gla_maps"), h + 1)
                        if h >= 2:
                            act.wait_ge(S("gla_pv"), h - 1)
                        act.activation(at_[:, h % 2, P:2 * P], PS[:, 4 + h % 2, P:2 * P], ACT.Copy)\
                           .then_inc(S("gla_cross"), 1)
                    act.wait_ge(S("gla_pv"), 4)
                    act.wait_ge(S("mix_done"), 2)
                    st.then(act.activation(osb, bank2(3), ACT.Copy))
                    act.activation(osq, osb, ACT.Square).then_inc(S("gla_sq"), 1)
                    act.wait_ge(S("gla_sum"), 1)
                    act.activation(ors, bank2(6), ACT.Sqrt, scale=1.0 / 64, bias=epst[:, 0:1])\
                       .then_inc(S("gla_root"), 1)
                    act.wait_ge(S("gla_ops"), 1)
                    act.activation(Ef, fq, ACT.Square).then_inc(S("fox_qk_sq"), 1)
                    act.activation(Eg, fk, ACT.Square).then_inc(S("fox_qk_sq"), 1)
                    act.wait_ge(S("fox_qk_sum"), 2)
                    for c in range(2):
                        act.activation((Ef, Eg)[c], bank2(4 + c), ACT.Sqrt, scale=1.0 / 64, bias=epst[:, 0:1])\
                           .then_inc(S("fox_qk_root"), 1)
                    act.wait_ge(S("mix_done"), 3)
                    soft_act(act, fox, {7: (osb, bank2(2))})
                    act.wait_ge(S("fox_o_out"), 1)
                    act.activation(osq, osb, ACT.Square).then_inc(S("fox_sq"), 1)
                    act.wait_ge(S("fox_sum"), 1)
                    act.activation(ors, bank2(6), ACT.Sqrt, scale=1.0 / 64, bias=epst[:, 0:1])\
                       .then_inc(S("fox_root"), 1)
                    ffn_act_all(act, "ffn2_", c_ffn2, S("mixo_x_ready"))

                @block.vector
                def _(dve):
                    st = Step(dve, S("dve_step"))
                    dve.wait_ge(S("cols_turn"), 1)
                    dve.tensor_copy(pcol[:, 0:NROW1], bank(0, NROW1)).then_inc(S("cols"), 1)
                    dve.wait_ge(S("cols"), 1)
                    ffn_dve_all(dve, "ffn1_", c_ffn1, COL1["ffn1_norm"], None)
                    norm_dve(dve, "mix_")
                    scaled_dve(dve, "mix_", hT, xT, COL1["mix_norm"], True)
                    dve.wait_ge(S("tok_psum"), 1)
                    dve.wait_ge(S("small"), 16 * 10)
                    st.then(dve.tensor_tensor(tz, PS[:, 6, 0:16].rearrange("p (t n) -> p t n", t=2), tb, ALU.add))
                    st.then(dve.tensor_scalar(tz[:, :, 0:4], tz[:, :, 0:4], -1.0, None, ALU.mult))
                    dve.tensor_copy(ta, tz).then_inc(S("tok_z"), 1)
                    dve.tensor_copy(dcol[0:64, :], tD[0:64, :].rearrange("p (c h) -> p h c", h=2)[:, 0, :])
                    st.then(dve.tensor_copy(dcol[64:128, :],
                                            tD[64:128, :].rearrange("p (c h) -> p h c", h=2)[:, 1, :]))
                    for c in range(6):
                        src = (xp, Bp, Cp)[c // 2][:, c % 2, :]
                        dst = (xs, Bc, Cc)[c // 2][:, c % 2, :]
                        if c % 2 == 0:
                            dve.wait_ge(S("proj_out"), 4 + c // 2)
                        w0 = COL1["ssm_conv_w"] + c
                        st.then(dve.tensor_scalar(dst, src[:, PAD:PAD + T], pcol[:, w0 + 18:w0 + 19], None, ALU.mult))
                        for j in range(3):
                            m = dve.scalar_tensor_tensor(dst, src[:, PAD - 3 + j:PAD - 3 + j + T],
                                                         pcol[:, w0 + 6 * j:w0 + 6 * j + 1], dst, ALU.mult, ALU.add)
                            if j < 2:
                                st.then(m)
                        m.then_inc(S("conv_acc"), 1)
                    dve.wait_ge(S("proj_out"), 12)
                    st.then(dve.tensor_tensor(cp[:, :, PAD:PAD + T], dc, dv, ALU.mult))
                    for c in range(2):
                        w0 = COL1["sc_conv_w"] + c
                        st.then(dve.tensor_scalar(cc[:, c, :], cp[:, c, PAD:PAD + T], pcol[:, w0 + 4:w0 + 5], None,
                                                  ALU.mult))
                        for j in range(2):
                            st.then(dve.scalar_tensor_tensor(cc[:, c, :], cp[:, c, PAD - 2 + j:PAD - 2 + j + T],
                                                             pcol[:, w0 + 2 * j:w0 + 2 * j + 1], cc[:, c, :],
                                                             ALU.mult, ALU.add))
                    dve.tensor_tensor(db, db, cc, ALU.mult).then_inc(S("sc_y"), 1)
                    dve.wait_ge(S("gate_ln"), 1)
                    st.then(dve.tensor_scalar(za, zg, 0.0, None, ALU.min))
                    st.then(dve.tensor_tensor(za, za, Ef, ALU.subtract))
                    st.then(dve.tensor_scalar(za, za, 1.0 / 16.0, None, ALU.mult))
                    for m in (1, 2, 4, 8, 16, 32):
                        first, second = halves(za, m)
                        st.then(dve.tensor_tensor(second, second, last_of(first, m), ALU.add))
                    first, second = halves(za, 64)
                    dve.tensor_tensor(K64.rearrange("p a b n -> p (a b) n"), last_of(first, 64), first, ALU.subtract)\
                       .then_inc(S("gla_pref"), 1)
                    dve.wait_ge(S("gla_exp"), 1)
                    st.then(dve.tensor_tensor(second, second, last_of(first, 64), ALU.add))
                    dve.tensor_tensor(K128, za[:, :, P - 1:P].broadcast_to([P, 2, P]), za[:, :, 0:P], ALU.subtract)\
                       .then_inc(S("gla_pref"), 1)
                    dve.wait_ge(S("tok_ln"), 1)
                    dve.wait_ge(S("A_exp"), 1)
                    st.then(dve.tensor_scalar(ta, ta, 0.0, None, ALU.max))
                    st.then(dve.tensor_tensor(ta, ta, te, ALU.add))
                    st.then(dve.tensor_copy(te, ta))
                    st.then(dve.tensor_tensor(ta[:, :, 4:8], ta[:, :, 4:8], over(tA, 2), ALU.mult))
                    dve.tensor_scalar(ta[:, :, 4:8], ta[:, :, 4:8], -1.0, None, ALU.mult).then_inc(S("tok_vals"), 1)
                    dve.wait_ge(S("tok_vals"), 1)
                    for t in range(2):
                        for h in range(8):
                            dve.tensor_scalar(bcs[:, t, h, :], ones[:], ta[:, t, h:h + 1], None, ALU.mult)\
                               .then_inc(S("bcs"), 1)
                    dve.wait_ge(S("acs_psum"), 1)
                    st.then(dve.tensor_copy(acs, PS[:, 6, 32:40].rearrange("p (t n) -> p t n", t=2)))
                    dve.wait_ge(S("xs_turn"), 1)
                    dve.tensor_tensor(xd.rearrange("p t (h n) -> p t h n", h=4),
                                      bank2(0).rearrange("p t (h n) -> p t h n", h=4),
                                      te[:, :, 4:8].unsqueeze(3).broadcast_to([P, 2, 4, 64]), ALU.mult)\
                       .then_inc(S("xd"), 1)
                    for g in range(2):
                        dve.wait_ge(S("cb_psum"), g + 1)
                        dve.tensor_tensor(Gm[:, g, :], PS[:, 1 + g, 0:3 * P], upper[:], ALU.mult)\
                           .then_inc(S("cb_masked"), 1)
                    for h in range(5):
                        if h < 4:
                            dve.wait_ge(S("acs_row"), h + 1)
                            if h >= 2:
                                dve.wait_ge(S("ssd_pv"), h - 1)
                            b = 4 + h % 2
                            dve.tensor_scalar(Lm[:, h % 2, 0:T], PS[:, b, 0:T], acs[:, 0, h:h + 1], 0.0,
                                              ALU.subtract, ALU.min)
                            dve.tensor_scalar(Lm[:, h % 2, T:T + P], PS[:, b, P:T], acs[:, 1, h:h + 1], 0.0,
                                              ALU.subtract, ALU.min).then_inc(S("seg"), 1)
                        if h >= 1:
                            g = h - 1
                            dve.wait_ge(S("seg_exp"), g + 1)
                            dve.wait_ge(S("cb_masked"), 2)
                            dve.tensor_tensor(Lm[:, g % 2, :], Lm[:, g % 2, :], Gm[:, g // 2, :], ALU.mult)\
                               .then_inc(S("ssd_w"), 1)
                    dve.wait_ge(S("ssd_pv"), 4)
                    for c in range(2):
                        st.then(dve.scalar_tensor_tensor(osb[:, c, :], xs[:, c, :],
                                                         dcol[:, c:c + 1],
                                                         bank2(3)[:, c, :], ALU.mult, ALU.add))
                    dve.wait_ge(S("proj_out"), 14)
                    dve.tensor_tensor(osb, osb, sz, ALU.mult).then_inc(S("ssd_y"), 1)
                    head_norm(dve, st, "ssd_root", osb, COL1["ssm_norm"], 4, None)
                    head_norm(dve, st, "sc_root", db, COL1["sc_out_norm"], 6, None)
                    dve.wait_ge(S("gla_exp"), 2)
                    st.then(dve.tensor_tensor(Kd, gk, Eg, ALU.mult))
                    st.then(dve.tensor_tensor(Qd, gq, Ef, ALU.mult))
                    k64 = K64.rearrange("p a b n -> p (a b) n")
                    st.then(dve.tensor_tensor(k64, halves(gk, 64)[0], k64, ALU.mult))
                    st.then(dve.tensor_tensor(K128, gk[:, :, 0:P], K128, ALU.mult))
                    dve.tensor_tensor(Q128, gq[:, :, P:T], Q128, ALU.mult).then_inc(S("gla_ops"), 1)
                    for h in range(4):
                        dve.wait_ge(S("gla_maps"), h + 1)
                        if h >= 2:
                            dve.wait_ge(S("gla_pv"), h - 1)
                        dve.wait_ge(S("gla_cross"), h + 1)
                        b = 4 + h % 2
                        for t in range(2):
                            c = 2 * t * P
                            dve.tensor_tensor(at_[0:64, h % 2, c:c + 64], PS[0:64, b, c:c + 64], upper[0:64, 0:64],
                                              ALU.mult)
                            dve.tensor_copy(at_[0:64, h % 2, c + 64:c + P], PS[0:64, b, c + 64:c + P])
                            m = dve.tensor_tensor(at_[64:128, h % 2, c + 64:c + P], PS[64:128, b, c + 64:c + P],
                                                  upper[64:128, 64:128], ALU.mult)
                        m.then_inc(S("gla_w"), 1)
                    head_norm(dve, st, "gla_root", osb, COL1["gla_norm"], 0, gg)
                    dve.wait_ge(S("fox_qk_root"), 2)
                    for c, (a, r, g) in enumerate(((fq, Ef, "fox_q_norm"), (fk, Eg, "fox_k_norm"))):
                        st.then(dve.reciprocal(r, r))
                        m = dve.scalar_tensor_tensor(a, a, pcol[:, COL1[g]:COL1[g] + 1], r, ALU.mult, ALU.mult)
                        if c == 0:
                            st.then(m)
                            m = dve.tensor_scalar(a, a, 0.125, None, ALU.mult)
                        m.then_inc(S("fox_qk"), 1)
                    soft_dve(dve, st, fox)
                    head_norm(dve, st, "fox_root", osb, COL1["fox_out_norm"], 2, None)
                    residual_dve(dve, "mixo_", c_out)
                    ffn_dve_all(dve, "ffn2_", c_ffn2, COL1["ffn2_norm"], S("mixo_x_ready"))

            clear_signals()
        end_part()

        take = carve()
        memT = take(KD, T)
        rmem = take(T)
        cosT, sinT = take(T), take(T)
        dmask1, dmask0 = take(3 * T), take(3 * P)
        lmask = take(7, 64)
        lb01, lbc = take(2, KD), take(2, KD)
        base = take.at[0]
        aq, ak = take(12, T), take(12, T)
        av = take(2, AW)
        hq, hk, hP = take(KD, T), take(KD, T), take(KD, T)
        hv = take(2, D)
        hog = take(KD, T)
        X = take(8, 2, T)
        hat, a128 = take(2, P), take(2, P)
        Xf = X.rearrange("p l h t -> p (l h t)")
        yat = Xf[:, 0:1024].rearrange("p (k t) -> p k t", k=4)
        xa, xb = (Xf[:, 2048 * i:2048 * (i + 1)].rearrange("p (k t) -> p k t", k=KD) for i in range(2))
        mt = work[:, 3072:3968].rearrange("p (b l n) -> p b l n", b=2, l=7)
        rp = sq[:].rearrange("p k t -> p (k t)").rearrange("p (b s f t) -> p b s f t", b=2, s=2, f=2)
        take.at[0] = base
        sgA, sgB, mg, brt = take(KD, T), take(KD, T), take(KD, T), take(2, T)
        take.at[0] = base
        memn, kx, qx, ox = (take(KD, T) for _ in range(4))
        vx = take(2, D)

        with nc.Block() as block:
            min_ = hT[:].rearrange("p k t -> p (k t)").rearrange("p (a n) -> p a n", a=TT)
            posi = work[:, 0:T].bitcast(I32)
            ang, nf, rr = work[:, T:2 * T], work[:, 2 * T:3 * T], work[:, 3 * T:4 * T]
            ni = work[:, 4 * T:5 * T].bitcast(I32)
            iot = work[:, 5 * T:6 * T].bitcast(I32)
            low = work[:, 6 * T:7 * T].bitcast(I32)
            invf = work[:, 7 * T:7 * T + 1]
            lbm = work[:, 8 * T:8 * T + 8]

            @block.sync
            def _(sp):
                sp.dma_start(min_, A["mem_2"][0].rearrange("(a p) n -> p a n", p=P)).then_inc(S("mem_in"), 16)
                sp.dma_start(posi, A["positions_2"][0].partition_broadcast(P)).then_inc(S("rope_in"), 16)
                sp.dma_start(invf, A["inv_freq"].rearrange("(p a) -> p a", a=1)).then_inc(S("rope_in"), 16)
                for l in range(DEPTH):
                    sp.dma_start(prow[8 * l:8 * l + 8, :], A["hgrn_lower_bounds_2"][l]
                                 .rearrange("(k p) -> k p", p=P)).then_inc(S("rows"), 16)

            @block.gpsimd
            def _(pool):
                st = Step(pool, S("pool_step"))
                pool.iota(iot, pattern=[[-1, T]], base=384, channel_multiplier=1).then_inc(S("iota"), 1)
                st.then(pool.memset(lmask, 0.0))
                for c in range(2):
                    q = slice(64 * c, 64 * c + 64)
                    st.then(pool.affine_select(out=lmask[q, 0, :], in_=lmask[q, 0, :], compare_op=ALU.not_equal,
                                               fill=1.0, base=0, pattern=[[-1, 64]], channel_multiplier=1))
                    for l in range(6):
                        m = 1 << l
                        v = lmask[q, l + 1, :].rearrange("p (b h m) -> p b h m", h=2, m=m)[:, :, 1, :]
                        st.then(pool.memset(v, 1.0))
                        st.then(pool.affine_select(out=v, in_=v, compare_op=ALU.is_ge, fill=0.0, base=0,
                                                   pattern=[[-2 * m, 32 // m], [0, m]], channel_multiplier=1))
                        st.then(pool.affine_select(out=v, in_=v, compare_op=ALU.is_ge, fill=0.0, base=m - 1,
                                                   pattern=[[2 * m, 32 // m], [0, m]], channel_multiplier=-1))
                st.then(pool.memset(dmask1[:, 0:T], 0.0))
                pool.wait_ge(S("dil"), 2)
                d3 = dmask1.rearrange("p (g n) -> p g n", g=3)
                st.then(pool.affine_select(out=d3, in_=d3, compare_op=ALU.is_ge, fill=NEG, base=P,
                                           pattern=[[0, 3], [-1, T]], channel_multiplier=1))
                st.then(pool.affine_select(out=dmask1[:, 0:T], in_=dmask1[:, 0:T], compare_op=ALU.is_ge, fill=NEG,
                                           base=0, pattern=[[1, T]], channel_multiplier=-1))
                pool.tensor_copy(dmask0.rearrange("p (g n) -> p g n", g=3), d3[:, :, P:T])\
                    .then_inc(S("dmasks"), 1)

            @block.tensor
            def _(pe):
                pe.wait_ge(S("mem_in"), 16)
                for k in range(KD):
                    for a in range(TT):
                        m = pe.transpose(bank2(k // 2)[:, k % 2, a * P:(a + 1) * P], min_[:, a, k * P:(k + 1) * P],
                                         ident[:])
                    m.then_inc(S("mem_turn"), 1)
                pe.wait_ge(S("rows"), 32)
                pe.transpose(bank(5, 16), prow[0:16, :], ident[0:16, 0:16]).then_inc(S("lb_turn"), 1)
                norm_pe(pe, "mem_")

            @block.scalar
            def _(act):
                norm_act(act, "mem_", memT, S("mem_out"))
                act.wait_ge(S("lb_z"), 1)
                act.activation(lb01, lb01, ACT.Exp).then_inc(S("lb_exp"), 1)
                act.wait_ge(S("angles"), 1)
                act.activation(sinT, rr, ACT.Sin).then_inc(S("tables"), 1)
                act.activation(cosT, nf, ACT.Sin).then_inc(S("tables"), 1)

            @block.vector
            def _(dve):
                st = Step(dve, S("dve_step"))
                dve.wait_ge(S("iota"), 1)
                for g, m in ((1, 3), (2, 15)):
                    st.then(dve.tensor_scalar(low, iot, m, None, ALU.bitwise_and))
                    st.then(dve.tensor_scalar(nf, low, 1.0, NEG, ALU.min, ALU.mult))
                    dve.tensor_copy(dmask1[:, g * T:(g + 1) * T], nf).then_inc(S("dil"), 1)
                    dve.wait_ge(S("dil"), g)
                for j in range(4):
                    dve.wait_ge(S("mem_turn"), 2 * j + 2)
                    dve.tensor_copy(memT[:, 2 * j:2 * j + 2, :], bank2(j)).then_inc(S("mem_out"), 1)
                dve.wait_ge(S("lb_turn"), 1)
                st.then(dve.tensor_copy(lb01, bank(5, 16).rearrange("p (l k) -> p l k", l=2)))
                st.then(dve.tensor_tensor(lbm, lb01[:, 0, :], lb01[:, 1, :], ALU.max))
                dve.tensor_tensor(lb01, lb01, over(lbm, 2), ALU.subtract).then_inc(S("lb_z"), 1)
                dve.wait_ge(S("lb_exp"), 1)
                st.then(dve.tensor_tensor(lbm, lb01[:, 0, :], lb01[:, 1, :], ALU.add))
                st.then(dve.reciprocal(lbm, lbm))
                st.then(dve.tensor_tensor(lb01[:, 1, :], lb01[:, 1, :], lbm, ALU.mult))
                st.then(dve.memset(lb01[:, 0, :], 0.0))
                dve.wait_ge(S("rope_in"), 32)
                st.then(dve.tensor_copy(ang, posi))
                st.then(dve.tensor_scalar(ang, ang, invf, None, ALU.mult))
                st.then(dve.tensor_scalar(nf, ang, 1.0 / (2.0 * np.pi), None, ALU.mult))
                st.then(dve.tensor_copy(ni, nf))
                st.then(dve.tensor_copy(nf, ni))
                c1 = 6.28125
                c2 = float(np.float32(2.0 * np.pi - c1) - np.float32(2.0 * np.pi - c1) % np.float32(2.0 ** -20))
                for c in (c1, c2, 2.0 * np.pi - c1 - c2):
                    st.then(dve.scalar_tensor_tensor(ang, nf, -c, ang, ALU.mult, ALU.add))
                PI = 3.1415925
                st.then(dve.tensor_scalar(rr, ang, -PI, PI, ALU.max, ALU.min))
                st.then(dve.tensor_scalar(ang, rr, -1.0, None, ALU.mult))
                st.then(dve.tensor_tensor(nf, ang, rr, ALU.max))
                dve.tensor_scalar(nf, nf, -1.0, float(np.pi / 2), ALU.mult, ALU.add).then_inc(S("angles"), 1)
                norm_dve(dve, "mem_")
                st.then(dve.tensor_copy(rmem, rstd[:]))

        clear_signals()
        end_part()

        with nc.Fori(0, DEPTH) as layer:
            W = {n: A[n + "_2"][layer] for n in ("ffn1_w_gu", "ffn1_w_down", "ffn2_w_gu", "ffn2_w_down", "w_in",
                                                 "w_att_branch", "w_hgrn_branch", "w_mix_out", "xattn_wq",
                                                 "xattn_wkv", "xattn_wo")}
            c_ffn1, c_proj = 0, 3 * NF
            c_gate = c_proj + len(PROJ2)
            c_att = c_gate + len(GATES)
            c_hg = c_att + 4
            c_mix = c_hg + 4
            c_kv = c_mix + 4
            c_q = c_kv + 8
            c_xo = c_q + 4
            c_ffn2 = c_xo + 4
            idx = {(name, c): n for n, (name, _, _, c) in enumerate(PROJ2)}
            evens = [CW * c for c in range(4)]

            att_units = []
            for h in range(4):
                for t in range(2):
                    def score(pe, a, h=h, t=t):
                        w = P * (t + 1)
                        for g in range(3):
                            m = pe.matmul(a[:, g * w:(g + 1) * w], aq[:, 4 * g + h, t * P:(t + 1) * P],
                                          ak[:, 4 * g + h, 0:w], start=True, stop=True, skip_group_check=True)
                        return m

                    def pv(pe, w, h=h, t=t):
                        o = bank2(2 + h // 2)[:, h % 2, t * P:(t + 1) * P]
                        n = 3 * (t + 1)
                        for j in range(n):
                            g, kt = j // (t + 1), j % (t + 1)
                            m = pe.matmul(o, av[:, kt, (4 * g + h) * P:(4 * g + h + 1) * P],
                                          w[:, j * P:(j + 1) * P], start=(j == 0), stop=(j == n - 1),
                                          skip_group_check=True)
                        return m
                    att_units.append({"n": 3 * P * (t + 1), "mask": (dmask0, dmask1)[t], "score": score, "pv": pv})
            att = Soft("att_", att_units, 4, float(P) ** -0.5)

            x_units = []
            for h in range(4):
                for t in range(2):
                    def score(pe, a, h=h, t=t):
                        for k in range(2):
                            m = pe.matmul(a[:, 0:T], qx[:, 2 * h + k, t * P:(t + 1) * P], kx[:, 2 * h + k, :],
                                          start=(k == 0), stop=(k == 1), skip_group_check=True)
                        return m

                    def pv(pe, w, h=h, t=t):
                        for d in range(2):
                            for j in range(2):
                                m = pe.matmul(bank2(2 + h % 2)[:, d, t * P:(t + 1) * P],
                                              vx[:, j, (2 * h + d) * P:(2 * h + d + 1) * P],
                                              w[:, j * P:(j + 1) * P], start=(j == 0), stop=(j == 1),
                                              skip_group_check=True)
                        return m
                    x_units.append({"n": T, "mask": None, "score": score, "pv": pv})
            xatt = Soft("xat_", x_units, 2, 1.0 / 16.0)

            with nc.Block() as block:
                @block.sync
                def _(sp):
                    for name, n in ROWS2:
                        r0 = COL2[name]
                        sp.dma_start(prow[r0:r0 + n, :], A[name][layer].rearrange("(k p) -> k p", p=P))\
                          .then_inc(S("rows"), 16)

                    def ffn(c0, p):
                        ffn_sp(sp, c0, W[p + "_w_gu"][:, 0:DFF], W[p + "_w_gu"][:, DFF:2 * DFF], W[p + "_w_down"])
                    ffn(c_ffn1, "ffn1")
                    gemm_sp(sp, c_proj, colchunks(W["w_in"], [o for _, o, _, _ in PROJ2 + GATES]))
                    gemm_sp(sp, c_att, colchunks(W["w_att_branch"], evens), 4)
                    gemm_sp(sp, c_hg, colchunks(W["w_hgrn_branch"], evens))
                    gemm_sp(sp, c_mix, colchunks(W["w_mix_out"], evens))
                    gemm_sp(sp, c_kv, colchunks(W["xattn_wkv"], [CW * c for c in range(8)]))
                    gemm_sp(sp, c_q, colchunks(W["xattn_wq"], evens))
                    gemm_sp(sp, c_xo, colchunks(W["xattn_wo"], evens))
                    ffn(c_ffn2, "ffn2")

                @block.gpsimd
                def _(pool):
                    pool.memset(hat[64:P, :, 0:64], 0.0).then_inc(S("pool_zero"), 1)

                def proj_pe(pe, n0, n1):
                    for n in range(n0, n1):
                        w = chunk(c_proj + n, KD, CW)
                        wait_chunk(pe, c_proj + n)
                        if n >= 4:
                            pe.wait_ge(S("proj_out"), n - 3)
                        for f in range(2):
                            for k in range(KD):
                                if n == 0 and f == 0:
                                    pe.wait_ge(S("mix_in_ready"), k + 1)
                                a, b = ((w[:, k, f * P:(f + 1) * P], hT[:, k, :]) if PROJ2[n][2] == "F" else
                                        (hT[:, k, f * P:(f + 1) * P], w[:, k, :]))
                                m = pe.matmul(bank2(n % 4)[:, f, :], a, b, start=(k == 0), stop=(k == KD - 1))
                        m.then_inc(S("chunk_done"), 1)

                @block.tensor
                def _(pe):
                    pe.sem_inc(S("chunk_done"), RING)
                    pe.wait_ge(S("rows"), 16 * len(ROWS2))
                    pe.transpose(bank(0, NROW2), prow[0:NROW2, :], ident[0:NROW2, 0:NROW2])\
                      .then_inc(S("cols_turn"), 1)
                    pe.wait_ge(S("cols"), 1)
                    ffn_pe_all(pe, "ffn1_", c_ffn1)
                    norm_pe(pe, "mix_")
                    proj_pe(pe, 0, 16)
                    for g in range(4):
                        proj_pe(pe, 16 + 3 * g, 19 + 3 * g)
                        pe.wait_ge(S("lev"), 16 * (g + 1))
                        pe.wait_ge(S("pool_zero"), 1)
                        for v in range(5):
                            u = 4 * g + v
                            if v < 4:
                                h, t = 2 * g + v // 2, v % 2
                                hl = v // 2
                                b = 4 + u % 2
                                if u >= 2:
                                    pe.wait_ge(S("hg_masked"), u - 1)
                                for c in range(2):
                                    o = t * P + 64 * c
                                    for l in range(7):
                                        ks, qs = ((hk[:, h, o:o + 64], hq[:, h, o:o + 64]) if l == 0 else
                                                  (X[:, l - 1, hl, o:o + 64], X[:, l - 1, hl, o:o + 64]))
                                        pe.matmul(PS[64 * c:64 * c + 64, b, 64 * l:64 * l + 64], ks, qs, start=True,
                                                  stop=True, skip_group_check=True)
                                o = t * P
                                m = pe.matmul(PS[0:64, b, 448:512], X[:, 6, hl, o:o + 64], X[:, 6, hl, o + 64:o + P],
                                              start=True, stop=True, skip_group_check=True)
                                if t == 1:
                                    if u > 1:
                                        pe.wait_ge(S("hg_copied"), u // 2)
                                    m = pe.matmul(PS[:, 6, P * (hl % 2):P * (hl % 2) + P], X[:, 7, hl, 0:P],
                                                  X[:, 7, hl, P:T], start=True, stop=True, skip_group_check=True)
                                m.then_inc(S("hg_maps"), 1)
                            if v >= 1:
                                w = u - 1
                                h, t = 2 * g + (v - 1) // 2, (v - 1) % 2
                                pe.wait_ge(S("hg_masked"), w + 1)
                                if t == 1:
                                    pe.wait_ge(S("hg_copied"), w // 2 + 1)
                                if v == 1 and g:
                                    pe.wait_ge(S("hg_o"), g)
                                o = bank2(7)[:, h % 2, t * P:(t + 1) * P]
                                vv = hv[:, :, h * P:(h + 1) * P]
                                if t == 1:
                                    pe.matmul(o, vv[:, 0, :], a128[:, w // 2 % 2, :], start=True, stop=False,
                                              skip_group_check=True)
                                pe.matmul(o, vv[:, t, :], hat[:, w % 2, :], start=(t == 0), stop=True,
                                          skip_group_check=True).then_inc(S("hg_pv"), 1)
                    proj_pe(pe, 28, 34)
                    for b in range(4):
                        pe.wait_ge(S("hg_sq"), 1)
                        pe.matmul(bank(4 + b), ones[:], Xf[:, 512 * b:512 * b + 512], start=True, stop=True)\
                          .then_inc(S("hg_sum"), 1)
                    pe.wait_ge(S("rope"), 12)
                    pe.wait_ge(S("proj_out"), 34)
                    pe.wait_ge(S("hg_root"), 4)
                    soft_pe(pe, att, lambda v: 0)
                    pe.wait_ge(S("att_o_out"), 2)
                    gemm_pe(pe, c_gate, "F" * 8, hT, "gate_out")
                    pe.wait_ge(S("gate_out"), 8)
                    gemm_pe(pe, c_att, "FFFF", yat, "none", k_=4)
                    pe.wait_ge(S("hg_done"), 1)
                    for n in range(4):
                        pe.wait_ge(S("branch_out"), n + 1)
                        gemm_pe1(pe, c_hg + n, n, hq)
                    pe.wait_ge(S("branch_out"), 8)
                    gemm_pe(pe, c_mix, "FFFF", mg, "none")
                    pe.wait_ge(S("mem_in_ready"), 8)
                    for n in range(8):
                        if n < 4:
                            pe.wait_ge(S("mixo_x_ready"), n + 1)
                        else:
                            pe.wait_ge(S("kv_out"), n - 3)
                        gemm_pe1(pe, c_kv + n, n % 4, memn, "F" if n < 4 else "T")
                    norm_pe(pe, "xa_")
                    pe.wait_ge(S("xa_in_ready"), 8)
                    for n in range(4):
                        pe.wait_ge(S("kv_out"), 5 + n)
                        gemm_pe1(pe, c_q + n, n, hT)
                    pe.wait_ge(S("q_out"), 4)
                    soft_pe(pe, xatt, lambda v: v // 2 - 1 if v % 2 == 0 and v >= 4 else 0)
                    pe.wait_ge(S("xat_o_out"), 4)
                    gemm_pe(pe, c_xo, "FFFF", ox, "none")
                    ffn_pe_all(pe, "ffn2_", c_ffn2)

                def proj_act(act, n0, n1):
                    for n in range(n0, n1):
                        name, _, _, c = PROJ2[n]
                        src = bank2(n % 4)
                        act.wait_ge(S("chunk_done"), RING + c_proj + n + 1)
                        if name in ("aq", "ak"):
                            r = n - idx["aq", 0]
                            if r >= 2:
                                act.wait_ge(S("rope"), r - 1)
                            act.activation(rp[:, r % 2, 0], src, ACT.Copy)
                            act.activation(rp[0:64, r % 2, 1], src[64:128], ACT.Copy, scale=-1.0)
                            m = act.activation(rp[64:128, r % 2, 1], src[0:64], ACT.Copy)
                        elif name in ("i", "av"):
                            m = act.activation({"i": hv, "av": av}[name][:, :, CW * c:CW * (c + 1)], src, ACT.Copy)
                        else:
                            dst, f, s = {"f": (hP, ACT.Sigmoid, 1.0), "q": (hq, ACT.Copy, float(P) ** -0.5),
                                         "og": (hog, ACT.Silu, 1.0)}[name]
                            m = act.activation(dst[:, 2 * c:2 * c + 2, :], src, f, scale=s)
                        m.then_inc(S("proj_out"), 1)

                @block.scalar
                def _(act):
                    st = Step(act, S("act_step"))
                    ffn_act_all(act, "ffn1_", c_ffn1, None)
                    norm_act(act, "mix_", xT, S("ffn1_x_ready"))
                    proj_act(act, 0, 8)
                    act.wait_ge(S("f_split"), 1)
                    act.activation(xa, xa, ACT.Ln).then_inc(S("f_ln"), 1)
                    act.activation(xb, xb, ACT.Ln).then_inc(S("f_ln"), 1)
                    proj_act(act, 8, 16)
                    for g in range(4):
                        for l in range(8):
                            act.wait_ge(S("pre"), 8 * g + l + 1)
                            act.activation(X[:, l], X[:, l], ACT.Exp).then_inc(S("lev_exp"), 1)
                        proj_act(act, 16 + 3 * g, 19 + 3 * g)
                        for v in (1, 3):
                            u = 4 * g + v
                            act.wait_ge(S("hg_maps"), u + 1)
                            if u >= 4:
                                act.wait_ge(S("hg_pv"), u - 3)
                            act.activation(a128[:, u // 2 % 2, :], PS[:, 6, P * (v // 2):P * (v // 2) + P],
                                           ACT.Copy).then_inc(S("hg_copied"), 1)
                        act.wait_ge(S("hg_pv"), 4 * g + 4)
                        act.activation(hq[:, 2 * g:2 * g + 2, :], bank2(7), ACT.Copy).then_inc(S("hg_o"), 1)
                    act.wait_ge(S("hg_o"), 4)
                    act.activation(xa, hq, ACT.Square).then_inc(S("hg_sq"), 1)
                    proj_act(act, 28, 34)
                    for b in range(4):
                        act.wait_ge(S("hg_sum"), b + 1)
                        act.activation(Xf[:, 2048 + 512 * b:2560 + 512 * b], bank(4 + b), ACT.Sqrt, scale=1.0 / P,
                                       bias=epst[:, 0:1]).then_inc(S("hg_root"), 1)
                    soft_act(act, att, {3: (yat[:, 0:2, :], bank2(2)), 7: (yat[:, 2:4, :], bank2(3))})
                    for n in range(8):
                        act.wait_ge(S("chunk_done"), RING + c_gate + n + 1)
                        act.activation((sgA, sgB)[n // 4][:, 2 * (n % 4):2 * (n % 4) + 2, :], bank2(n % 4),
                                       ACT.Sigmoid).then_inc(S("gate_out"), 1)
                    for n in range(8):
                        act.wait_ge(S("chunk_done"), RING + c_kv + n + 1)
                        c = n % 4
                        dst = kx[:, 2 * c:2 * c + 2, :] if n < 4 else vx[:, :, CW * c:CW * (c + 1)]
                        act.activation(dst, bank2(c), ACT.Copy).then_inc(S("kv_out"), 1)
                    norm_act(act, "xa_", xT, S("mixo_x_ready"))
                    for n in range(4):
                        act.wait_ge(S("chunk_done"), RING + c_q + n + 1)
                        act.activation(qx[:, 2 * n:2 * n + 2, :], bank2(n), ACT.Copy).then_inc(S("q_out"), 1)
                    soft_act(act, xatt, {2 * h + 1: (ox[:, 2 * h:2 * h + 2, :], bank2(2 + h % 2)) for h in range(4)})
                    ffn_act_all(act, "ffn2_", c_ffn2, S("xo_x_ready"))

                def rope_dve(dve, st, r0, r1):
                    for r in range(r0, r1):
                        dve.wait_ge(S("proj_out"), idx["aq", 0] + r + 1)
                        raw, swp = rp[:, r % 2, 0], rp[:, r % 2, 1]
                        dst = (aq, ak)[r // 6][:, 2 * (r % 6):2 * (r % 6) + 2, :]
                        st.link(dve.tensor_tensor(raw, raw, over(cosT, 2), ALU.mult))
                        st.then(dve.tensor_tensor(swp, swp, over(sinT, 2), ALU.mult))
                        dve.tensor_tensor(dst, raw, swp, ALU.add).then_inc(S("rope"), 1)

                @block.vector
                def _(dve):
                    st = Step(dve, S("dve_step"))
                    dve.wait_ge(S("cols_turn"), 1)
                    dve.tensor_copy(pcol[:, 0:NROW2], bank(0, NROW2)).then_inc(S("cols"), 1)
                    dve.wait_ge(S("cols"), 1)
                    st.then(dve.tensor_copy(lbc[:, 0:1, :], lb01[:, bass.ds(layer, 1), :]))
                    st.then(dve.tensor_scalar(lbc[:, 1, :], lbc[:, 0, :], -1.0, 1.0, ALU.mult, ALU.add))
                    ffn_dve_all(dve, "ffn1_", c_ffn1, COL2["ffn1_norm_2"], None)
                    norm_dve(dve, "mix_")
                    scaled_dve(dve, "mix_", hT, xT, COL2["mix_norm_2"], True)
                    dve.wait_ge(S("proj_out"), 4)
                    for k in range(KD):
                        m = dve.tensor_scalar(hP[:, k, :], hP[:, k, :], lbc[:, 1, k:k + 1], lbc[:, 0, k:k + 1],
                                              ALU.mult, ALU.add)
                    st.then(m)
                    st.link(dve.tensor_scalar(hk, hP, -1.0, 1.0, ALU.mult, ALU.add))
                    st.link(dve.tensor_scalar(xa, hP, 2.0 ** -60, None, ALU.max))
                    dve.tensor_scalar(xb, hP, 2.0 ** -60, 2.0 ** 60, ALU.min, ALU.mult).then_inc(S("f_split"), 1)
                    dve.wait_ge(S("f_ln"), 2)
                    st.then(dve.tensor_tensor(hP, xa, xb, ALU.add))
                    dve.wait_ge(S("proj_out"), 8)
                    for g in range(4):
                        pr = hP[:, 2 * g:2 * g + 2, :]
                        if g:
                            dve.wait_ge(S("hg_pv"), 4 * g)
                        for l, m in enumerate(LEVELS):
                            first, second = halves(pr, m)
                            xf, xs_ = halves(X[:, l], m)
                            dve.tensor_tensor(xf, last_of(first, m), first, ALU.subtract)
                            dve.tensor_copy(xs_, second).then_inc(S("pre"), 1)
                            dve.wait_ge(S("pre"), 8 * g + l + 1)
                            if m < P:
                                st.then(dve.tensor_tensor(second, second, last_of(first, m), ALU.add))
                        for l, m in enumerate(LEVELS):
                            dve.wait_ge(S("lev_exp"), 8 * g + l + 1)
                            for half in range(2):
                                xh = halves(X[:, l], m)[half]
                                qk = halves((hk, hq)[half][:, 2 * g:2 * g + 2, :], m)[half]
                                dve.tensor_tensor(xh, xh, qk, ALU.mult).then_inc(S("lev"), 1)
                        rope_dve(dve, st, 3 * g, 3 * g + 3)
                        for v in range(4):
                            u = 4 * g + v
                            dve.wait_ge(S("hg_maps"), u + 1)
                            st.then(dve.tensor_tensor(mt[:, u % 2], PS[:, 4 + u % 2, 0:448]
                                                      .rearrange("p (l n) -> p l n", l=7), lmask, ALU.mult))
                            if u >= 2:
                                dve.wait_ge(S("hg_pv"), u - 1)
                            for c in range(2):
                                q = slice(64 * c, 64 * c + 64)
                                dve.tensor_reduce(hat[q, u % 2, q], mt[q, u % 2].rearrange("p l n -> p n l"), AX,
                                                  ALU.add)
                            dve.tensor_copy(hat[0:64, u % 2, 64:P], PS[0:64, 4 + u % 2, 448:512])\
                               .then_inc(S("hg_masked"), 1)
                    dve.wait_ge(S("hg_root"), 4)
                    st.then(dve.reciprocal(xb, xb))
                    for k in range(KD):
                        gc = COL2["hgrn_head_norm_2"] + k
                        m = dve.scalar_tensor_tensor(hq[:, k, :], hq[:, k, :], pcol[:, gc:gc + 1], xb[:, k, :],
                                                     ALU.mult, ALU.mult)
                    st.then(m)
                    dve.wait_ge(S("proj_out"), 16)
                    dve.tensor_tensor(hq, hq, hog, ALU.mult).then_inc(S("hg_done"), 1)
                    soft_dve(dve, st, att)
                    for n in range(8):
                        dve.wait_ge(S("chunk_done"), RING + c_att + n + 1)
                        dve.wait_ge(S("gate_out"), 8)
                        c = n % 4
                        m2 = mg[:, 2 * c:2 * c + 2, :]
                        if n < 4:
                            dve.tensor_tensor(m2, bank2(c), sgA[:, 2 * c:2 * c + 2, :], ALU.mult)\
                               .then_inc(S("branch_out"), 1)
                        else:
                            dve.wait_ge(S("branch_out"), n)
                            st.then(dve.tensor_tensor(brt, bank2(c), sgB[:, 2 * c:2 * c + 2, :], ALU.mult))
                            dve.tensor_tensor(m2, m2, brt, ALU.add).then_inc(S("branch_out"), 1)
                    residual_dve(dve, "mixo_", c_mix)
                    for k in range(KD):
                        gc = COL2["mem_norm_2"] + k
                        dve.scalar_tensor_tensor(memn[:, k, :], memT[:, k, :], pcol[:, gc:gc + 1], rmem, ALU.mult,
                                                 ALU.mult).then_inc(S("mem_in_ready"), 1)
                    norm_dve(dve, "xa_")
                    scaled_dve(dve, "xa_", hT, xT, COL2["xattn_norm_2"], True)
                    soft_dve(dve, st, xatt)
                    residual_dve(dve, "xo_", c_xo)
                    ffn_dve_all(dve, "ffn2_", c_ffn2, COL2["ffn2_norm_2"], S("xo_x_ready"))

            clear_signals()
        end_part()

        with nc.Block() as block:
            rows = sq[:].rearrange("p k t -> p (k t)").rearrange("p (a n) -> p a n", a=TT)

            @block.sync
            def _(sp):
                sp.dma_start(prow[0:8, :], A["final_norm_2"].rearrange("(k p) -> k p", p=P)).then_inc(S("rows"), 16)
                sp.wait_ge(S("rows_out"), 4)
                sp.dma_start(out[0].rearrange("(a p) n -> p a n", p=P), rows).then_inc(S("stored"), 16)
                sp.wait_ge(S("stored"), 16)

            @block.scalar
            def _(act):
                norm_act(act, "fin_", xT)

            @block.tensor
            def _(pe):
                pe.wait_ge(S("rows"), 16)
                pe.transpose(bank(0, 8), prow[0:8, :], ident[0:8, 0:8]).then_inc(S("cols_turn"), 1)
                norm_pe(pe, "fin_")
                for a in range(TT):
                    for k in range(KD):
                        if a == 0:
                            pe.wait_ge(S("fin_in_ready"), k + 1)
                        m = pe.transpose(PS[:, 2 * a + k // 4, (k % 4) * P:(k % 4 + 1) * P],
                                         hT[:, k, a * P:(a + 1) * P], ident[:])
                        if k % 4 == 3:
                            m.then_inc(S("row_turn"), 1)

            @block.vector
            def _(dve):
                dve.wait_ge(S("cols_turn"), 1)
                dve.tensor_copy(pcol[:, 0:8], bank(0, 8)).then_inc(S("cols"), 1)
                dve.wait_ge(S("cols"), 1)
                norm_dve(dve, "fin_")
                scaled_dve(dve, "fin_", hT, xT, 0, True)
                for j in range(4):
                    dve.wait_ge(S("row_turn"), j + 1)
                    dve.tensor_copy(rows[:, j // 2, 512 * (j % 2):512 * (j % 2) + 512], bank(j))\
                       .then_inc(S("rows_out"), 1)
        end_part()


_INS = ['x', 'ffn1_norm', 'ffn1_w_gate', 'ffn1_w_up', 'ffn1_w_down', 'mix_norm', 'w_in', 'gla_w_gate_up',
        'gla_b_gate', 'gla_norm', 'fox_b_forget', 'fox_q_norm', 'fox_k_norm', 'fox_out_norm', 'ssm_conv_w',
        'ssm_conv_b', 'ssm_dt_bias', 'ssm_A_log', 'ssm_D', 'ssm_norm', 'sc_conv_w', 'sc_out_norm', 'w_out',
        'ffn2_norm', 'ffn2_w_gate', 'ffn2_w_up', 'ffn2_w_down', 'mem_2', 'positions_2', 'ffn1_norm_2',
        'ffn1_w_gu_2', 'ffn1_w_down_2', 'mix_norm_2', 'w_in_2', 'hgrn_lower_bounds_2', 'hgrn_head_norm_2',
        'w_att_branch_2', 'w_hgrn_branch_2', 'w_mix_out_2', 'xattn_norm_2', 'mem_norm_2', 'xattn_wq_2',
        'xattn_wkv_2', 'xattn_wo_2', 'ffn2_norm_2', 'ffn2_w_gu_2', 'ffn2_w_down_2', 'final_norm_2']
_OUTS = [((1, T, D), 'float32')]


def kernel(**inputs):
    import numpy as _np
    import concourse.bacc as _bacc
    from concourse import mybir as _mybir
    from concourse.bass_utils import run_bass_kernel_spmd as _run

    nc = _bacc.Bacc("TRN2", target_bir_lowering=False, num_devices=1)
    arrays, args = {}, {}
    inv = (_np.float32(10000.0) ** (-_np.arange(0, P, 2, dtype=_np.float32) / _np.float32(P))).astype(_np.float32)
    consts = {"inv_freq": _np.concatenate([inv, inv])}
    for name in _INS + ["inv_freq"]:
        a = _np.ascontiguousarray(consts[name] if name in consts else inputs[name])
        arrays[f"in_{name}_dram"] = a
        args[name] = nc.dram_tensor(f"in_{name}_dram", a.shape, _mybir.dt.from_np(a.dtype),
                                    kind="ExternalInput").ap()
    (shape, dtype), = _OUTS
    out = nc.dram_tensor("out_0_dram", shape, _mybir.dt.from_np(_np.dtype(dtype)), kind="ExternalOutput").ap()
    build(nc, args, out)
    r = _run(nc, [arrays], core_ids=[0])
    return r.results[0]["out_0_dram"]
```

```python
from contextlib import ExitStack

import numpy as np

import concourse.bass as bass
from concourse import mybir

P = 128
T = 256
TT = T // P
D = 1024
KD = D // P
DFF = 2816
NF = DFF // T
DEPTH = 2
EPS = 1e-6
NEG = -1e30
RING = 6
CW = 256

ALU = mybir.AluOpType
ACT = mybir.ActivationFunctionType
AX = mybir.AxisListType.X
F32 = mybir.dt.float32
I32 = mybir.dt.int32

A_Q, A_K, A_V, A_G, A_LR = 0, 256, 512, 768, 1024
B_Q, B_K, B_V, B_F = 1040, 1296, 1552, 1808
C_Z, C_X, C_B, C_C, C_DT = 1812, 2068, 2324, 2580, 2836
D_B, D_C, D_V = 2840, 3096, 3352
PROJ1 = [("a_q", A_Q, "F"), ("xs", C_X, "F"), ("B", C_B, "F"), ("C", C_C, "F"), ("a_k", A_K, "F"),
         ("a_v", A_V, "T"), ("b_q", B_Q, "F"), ("b_k", B_K, "F"), ("b_v", B_V, "T"), ("c_z", C_Z, "F"),
         ("a_g", A_G, "F"), ("d_c", D_C, "F"), ("d_v", D_V, "F"), ("d_b", D_B, "F")]
AW = 3 * 512
H_Q, H_F, H_I, H_O = 3 * AW, 3 * AW + D, 3 * AW + 2 * D, 3 * AW + 3 * D
G_A, G_B = 3 * AW + 4 * D, 3 * AW + 5 * D
PROJ2 = ([("f", H_F + CW * c, "F", c) for c in range(4)] + [("q", H_Q + CW * c, "F", c) for c in range(4)]
         + [("i", H_I + CW * c, "T", c) for c in range(4)] + [("og", H_O + CW * c, "F", c) for c in range(4)]
         + [p for g in range(4) for p in
            [(("aq", "ak")[r // 6], AW * (r // 6) + CW * (r % 6), "F", r % 6) for r in range(3 * g, 3 * g + 3)]
            + [("av", 2 * AW + CW * g, "T", g)]]
         + [("av", 2 * AW + CW * c, "T", c) for c in (4, 5)])
GATES = [("gb", G_B + CW * c, "F", c) for c in range(4)] + [("ga", G_A + CW * c, "F", c) for c in range(4)]
CROSS = [("k", 0), ("k", 1), ("k", 2), ("k", 3), ("v", 0), ("q", 0),
         ("q", 1), ("v", 1), ("q", 2), ("v", 2), ("q", 3), ("v", 3)]
CROSS_AHEAD = 6
CROSS_FILL = {0: 6, 1: 7, 2: 8, 3: 9, 4: 10, 6: 11}

ROWS1 = [("ffn1_norm", 8), ("mix_norm", 8), ("ffn2_norm", 8), ("gla_b_gate", 2), ("gla_norm", 2),
         ("fox_out_norm", 2), ("ssm_conv_b", 6), ("ssm_norm", 2), ("sc_out_norm", 2),
         ("ssm_conv_w", 24), ("sc_conv_w", 6), ("fox_q_norm", 1), ("fox_k_norm", 1)]
ROWS2 = [("ffn1_norm_2", 8), ("mix_norm_2", 8), ("hgrn_head_norm_2", 8), ("xattn_norm_2", 8),
         ("mem_norm_2", 8), ("ffn2_norm_2", 8)]


def row_starts(rows):
    at, out = 0, {}
    for name, n in rows:
        out[name] = at
        at += n
    return out, at


COL1, NROW1 = row_starts(ROWS1)
COL2, NROW2 = row_starts(ROWS2)
LEVELS = [1, 2, 4, 8, 16, 32, 64, 128]


class Step:

    def __init__(self, eng, sem):
        self.eng, self.sem, self.n = eng, sem, 0

    def link(self, ins):
        ins.then_inc(self.sem, 1)
        self.n += 1

    def wait(self):
        if self.n:
            self.eng.wait_ge(self.sem, self.n)

    def then(self, ins):
        self.link(ins)
        self.wait()


def build(nc, A, out):
    with ExitStack() as ctx:
        def sb(name, shape, dt=F32):
            return ctx.enter_context(nc.sbuf_tensor(name, shape, dt))

        sems = {}
        scope = [ExitStack()]

        def S(name):
            if name not in sems:
                sems[name] = scope[0].enter_context(nc.semaphore(name))
            return sems[name]

        def clear_signals():
            with nc.Block() as block:
                @block.gpsimd
                def _(pool):
                    for s in sems.values():
                        pool.sem_clear(s)

        def end_part():
            scope[0].close()
            scope[0] = ExitStack()
            sems.clear()

        PS = ctx.enter_context(nc.psum_tensor("PS", [P, 8, 512], F32))

        xT = sb("xT", [P, KD, T])
        hT = sb("hT", [P, KD, T])
        ring = sb("ring", [P, RING, KD * CW])
        sq = sb("sq", [P, KD, T])
        rstd = sb("rstd", [P, T])
        ident = sb("ident", [P, P])
        ones = sb("ones", [P, P])
        ones64 = sb("ones64", [P, P])
        upper = sb("upper", [P, 3 * P])
        neg_causal = sb("neg_causal", [P, 2 * P])
        epst = sb("epst", [P, 1])
        prow = sb("prow", [P, P])
        cols1 = sb("cols1", [P, DEPTH, NROW1])
        cols2 = sb("cols2", [P, DEPTH, NROW2])
        pcol = sb("pcol", [P, P])
        work = sb("work", [P, 4096])
        g_sc, u_sc, s_sb, h_ff = (work[:, 1024 * i:1024 * (i + 1)].rearrange("p (b n) -> p b n", b=2)
                                  for i in range(4))
        soft_w, soft_t = (work[:, 1536 * i:1536 * (i + 1)].rearrange("p (b n) -> p b n", b=2) for i in range(2))
        soft_m = sb("soft_m", [P, 2, 4])
        zeros = sb("zeros", [P, P])
        ARENA = 28700
        arena = sb("arena", [P, ARENA])

        def carve():
            at = [0]

            def take(*shape, at_=None):
                n = int(np.prod(shape))
                a0 = at[0] if at_ is None else at_
                assert a0 + n <= ARENA, (a0, n)
                ap = arena[:, a0:a0 + n]
                if at_ is None:
                    at[0] += n
                if len(shape) == 1:
                    return ap
                names = "abcd"[:len(shape)]
                return ap.rearrange(f"p ({' '.join(names)}) -> p {' '.join(names)}",
                                    **{c: s for c, s in zip(names, shape)})
            take.at = at
            return take

        def bank(b, n=512):
            return PS[:, b, 0:n]

        def bank2(b):
            return PS[:, b, :].rearrange("p (a n) -> p a n", a=2)

        def over(ap, k):
            return ap.unsqueeze(1).broadcast_to([P, k, ap.shape[-1]])

        ahead = {stack: [ctx.enter_context(nc.semaphore(f"ahead{stack}_{j}")) for j in range(2)]
                 for stack in (1, 2)}

        def first_chunks(stack, layer):
            wg, wu = ((A["ffn1_w_gate"][layer], A["ffn1_w_up"][layer]) if stack == 1 else
                      (A["ffn1_w_gu_2"][layer][:, 0:DFF], A["ffn1_w_gu_2"][layer][:, DFF:2 * DFF]))
            return [w[:, 0:CW].rearrange("(k p) f -> p k f", p=P) for w in (wg, wu)]

        def load_ahead(sp, stack, layer, n_chunks=None):
            for j, src in enumerate(first_chunks(stack, layer)):
                if n_chunks is not None:
                    last_user = (n_chunks - 1 - j) // RING * RING + j
                    sp.wait_ge(S("chunk_done"), RING + last_user + 1)
                sp.dma_start(chunk(j, KD, CW), src).then_inc(ahead[stack][j], 16)


        def load_chunk(sp, n, src, dst_shape, i=0):
            sp.wait_ge(S("chunk_done"), n + 1 + i * RING)
            k, w = dst_shape
            dst = ring[:, n % RING, 0:k * w].rearrange("p (k w) -> p k w", k=k)
            sp.dma_start(dst, src).then_inc(S(f"landed{n % RING}"), 16)

        def chunk(n, k, w):
            return ring[:, n % RING, 0:k * w].rearrange("p (k w) -> p k w", k=k)

        def wait_chunk(pe, n, i=0):
            pe.wait_ge(S(f"landed{n % RING}"), 16 * (n // RING + 1) + i * 16)

        def norm_act(act, p, src, ready=None):
            for j in range(4):
                if ready:
                    act.wait_ge(ready, j + 1)
                act.activation(sq[:, 2 * j:2 * j + 2, :], src[:, 2 * j:2 * j + 2, :], ACT.Square)\
                   .then_inc(S(p + "squares"), 1)
            act.wait_ge(S(p + "sums"), 1)
            act.activation(rstd[:], bank(4, T), ACT.Sqrt, scale=1.0 / D, bias=epst[:, 0:1])\
               .then_inc(S(p + "root"), 1)

        def norm_add_dve(dve, p):
            for j in range(1, 4):
                dve.wait_ge(S(p + "squares"), j + 1)
                if j > 1:
                    dve.wait_ge(S(p + "added"), j - 1)
                dve.tensor_tensor(sq[:, 0:2, :], sq[:, 0:2, :], sq[:, 2 * j:2 * j + 2, :], ALU.add)\
                   .then_inc(S(p + "added"), 1)
            dve.wait_ge(S(p + "added"), 3)
            dve.tensor_tensor(sq[:, 0, :], sq[:, 0, :], sq[:, 1, :], ALU.add).then_inc(S(p + "added"), 1)

        def norm_pe(pe, p):
            pe.wait_ge(S(p + "added"), 4)
            pe.matmul(bank(4, T), ones[:], sq[:, 0, :], start=True, stop=True).then_inc(S(p + "sums"), 1)

        def norm_dve(dve, p):
            norm_add_dve(dve, p)
            dve.wait_ge(S(p + "root"), 1)
            dve.reciprocal(rstd[:], rstd[:]).then_inc(S(p + "rstd"), 1)
            dve.wait_ge(S(p + "rstd"), 1)

        def scaled_dve(dve, p, dst, src, gain, with_rstd, ready=None):
            for k in range(KD):
                if ready and k % 2 == 0:
                    dve.wait_ge(ready, k // 2 + 1)
                if with_rstd:
                    dve.scalar_tensor_tensor(dst[:, k, :], src[:, k, :], pcol[:, gain + k:gain + k + 1], rstd[:],
                                             ALU.mult, ALU.mult).then_inc(S(p + "in_ready"), 1)
                else:
                    dve.tensor_scalar(dst[:, k, :], src[:, k, :], pcol[:, gain + k:gain + k + 1], None,
                                      ALU.mult).then_inc(S(p + "in_ready"), 1)

        def ffn_sp(sp, c0, wg, wu, wd):
            def cols(w, s):
                return w[:, bass.ts(s, CW)].rearrange("(k p) f -> p k f", p=P)

            def rows(s):
                return wd[bass.ts(s, T), :].rearrange("(k p) f -> p k f", p=P)
            if c0:
                load_chunk(sp, c0, cols(wg, 0), (KD, CW))
                load_chunk(sp, c0 + 1, cols(wu, 0), (KD, CW))
            with sp.Fori(0, (NF - 1) // 2) as i:
                for j in range(2):
                    s = 2 * i + (1 + j)
                    n = c0 + 2 + 3 * j
                    load_chunk(sp, n, cols(wg, s), (KD, CW), i)
                    load_chunk(sp, n + 1, cols(wu, s), (KD, CW), i)
                    load_chunk(sp, n + 2, rows(s - 1), (2, D), i)
            load_chunk(sp, c0 + 3 * NF - 1, rows(NF - 1), (2, D))

        def ffn_pe(pe, p, c0, stack, layer):
            def up(n, b, i=0, first=False):
                w = chunk(n, KD, CW)
                wait_chunk(pe, n, i)
                for f in range(2):
                    for k in range(KD):
                        if first and f == 0:
                            pe.wait_ge(S(p + "in_ready"), k + 1)
                        m = pe.matmul(bank2(b)[:, f, :], w[:, k, f * P:(f + 1) * P], hT[:, k, :],
                                      start=(k == 0), stop=(k == KD - 1))
                m.then_inc(S("chunk_done"), 1)

            def down(n, b, i, hs, last):
                w = chunk(n, 2, D)
                wait_chunk(pe, n, i)
                pe.wait_ge(S(p + "hidden"), hs)
                for k in range(2):
                    for o in range(KD):
                        m = pe.matmul(bank2(4 + o // 2)[:, o % 2, :], w[:, k, o * P:(o + 1) * P],
                                      h_ff[:, b, k * T:(k + 1) * T],
                                      start=False, stop=(last and k == 1),
                                      skip_group_check=True)
                m.then_inc(S("chunk_done"), 1)

            for j in range(2):
                if c0 == 0:
                    pe.wait_ge(ahead[stack][j], 16 * layer + 16)
                    pe.sem_inc(S(f"landed{j}"), 16)
                up(c0 + j, 2 * j, first=(j == 0))
            norm_pe(pe, p)
            zero_sums_pe(pe, p)
            with pe.Fori(0, (NF - 1) // 2) as i:
                for j in range(2):
                    n = c0 + 2 + 3 * j
                    up(n, 1 - j, i)
                    up(n + 1, 3 - j, i)
                    down(n + 2, j, i, 2 * i + (1 + j), False)
            down(c0 + 3 * NF - 1, 0, 0, NF, True)

        def zero_sums_pe(pe, p):
            pe.wait_ge(S(p + "root"), 1)
            for b in range(4, 8):
                pe.matmul(bank(b, 2), zeros[:], zeros[:, 0:2], start=True, stop=False, skip_group_check=True)

        def ffn_act(act, p, c0):
            def silu(b, n_gs):
                act.wait_ge(S(p + "gate_scaled"), n_gs)
                act.activation(s_sb[:, b, :], g_sc[:, b, :], ACT.Silu).then_inc(S(p + "silu"), 1)
            silu(0, 1)
            with act.Fori(0, (NF - 1) // 2) as i:
                for j in range(2):
                    silu(1 - j, 2 * i + (2 + j))

        def ffn_dve(dve, p, c0):
            def step(b, s, n_done, n_prev_down):
                dve.wait_ge(S("chunk_done"), n_done)
                dve.tensor_tensor(g_sc[:, b, :].rearrange("p (a n) -> p a n", a=2), bank2(b), over(rstd[:], 2),
                                  ALU.mult).then_inc(S(p + "gate_scaled"), 1)
                dve.wait_ge(S("chunk_done"), n_done + 1)
                dve.tensor_tensor(u_sc[:, b, :].rearrange("p (a n) -> p a n", a=2), bank2(2 + b), over(rstd[:], 2),
                                  ALU.mult).then_inc(S(p + "up_scaled"), 1)
                dve.wait_ge(S(p + "up_scaled"), s + 1)
                dve.wait_ge(S(p + "silu"), s + 1)
                if n_prev_down is not None:
                    dve.wait_ge(S("chunk_done"), n_prev_down)
                dve.tensor_tensor(h_ff[:, b, :], s_sb[:, b, :], u_sc[:, b, :], ALU.mult)\
                   .then_inc(S(p + "hidden"), 1)
            step(0, 0, RING + c0 + 1, None)
            with dve.Fori(0, (NF - 1) // 2) as i:
                for j in range(2):
                    n = c0 + 2 + 3 * j
                    step(1 - j, 2 * i + (1 + j), i * RING + (RING + n + 1), i * RING + (RING + n))
            dve.wait_ge(S("chunk_done"), RING + c0 + 3 * NF)
            for j in range(4):
                x2 = xT[:, 2 * j:2 * j + 2, :]
                dve.scalar_tensor_tensor(x2, bank2(4 + j), 0.5, x2, ALU.mult, ALU.add)\
                   .then_inc(S(p + "x_ready"), 1)

        def gemm_sp(sp, c0, srcs, k=KD):
            for n, src in enumerate(srcs):
                load_chunk(sp, c0 + n, src, (k, CW))

        def gemm_pe(pe, c0, layouts, rhs, k_=KD):
            for n, lay in enumerate(layouts):
                w = chunk(c0 + n, k_, CW)
                b = n
                wait_chunk(pe, c0 + n)
                for f in range(2):
                    for k in range(k_):
                        if lay == "F":
                            m = pe.matmul(bank2(b)[:, f, :], w[:, k, f * P:(f + 1) * P], rhs[:, k, :],
                                          start=(k == 0), stop=(k == k_ - 1))
                        else:
                            m = pe.matmul(bank2(b)[:, f, :], rhs[:, k, f * P:(f + 1) * P], w[:, k, :],
                                          start=(k == 0), stop=(k == k_ - 1))
                m.then_inc(S("chunk_done"), 1)

        def gemm_pe1(pe, n, b, rhs, lay="F", kn=KD, ready=None):
            w = chunk(n, kn, CW)
            wait_chunk(pe, n)
            for f in range(2):
                for k in range(kn):
                    if ready and f == 0:
                        pe.wait_ge(ready, k + 1)
                    a, r = ((w[:, k, f * P:(f + 1) * P], rhs[:, k, :]) if lay == "F" else
                            (rhs[:, k, f * P:(f + 1) * P], w[:, k, :]))
                    m = pe.matmul(bank2(b)[:, f, :], a, r, start=(k == 0), stop=(k == kn - 1))
            m.then_inc(S("chunk_done"), 1)

        EARLY = 2

        def early_out_dve(dve, c0, dst):
            for n in range(EARLY):
                dve.wait_ge(S("chunk_done"), RING + c0 + n + 1)
                dve.tensor_tensor(dst[n], bank2(n), over(rstd[:], 2), ALU.mult).then_inc(S("early_out"), 1)

        def residual_dve(dve, p, c0):
            for n in range(4):
                dve.wait_ge(S("chunk_done"), RING + c0 + n + 1)
                x2 = xT[:, 2 * n:2 * n + 2, :]
                dve.tensor_tensor(x2, bank2(n), x2, ALU.add).then_inc(S(p + "x_ready"), 1)

        def colchunks(w, offs, kt=KD):
            return [w[:, o:o + CW].rearrange("(k p) f -> p k f", p=P) for o in offs]

        class Soft:
            def __init__(self, p, units, scale):
                self.p, self.units, self.scale = p, units, scale

            def area(self, u, n):
                a = PS[:, 4 + 2 * (u % 2):6 + 2 * (u % 2), :].rearrange("p a n -> p (a n)")
                return a[:, 0:n]

        def soft_pe(pe, sf, out_waits, between):
            U = len(sf.units)
            p = sf.p
            for u in range(U + 2):
                if u < U:
                    if u >= 2:
                        pe.wait_ge(S(p + "turned"), u - 1)
                    m = sf.units[u]["score"](pe, sf.area(u, sf.units[u]["n"]))
                    m.then_inc(S(p + "scores"), 1)
                between(u)
                if 1 <= u <= U:
                    v = u - 1
                    pe.wait_ge(S(p + "weights"), v + 1)
                    a = sf.area(v, sf.units[v]["n"])
                    for t in range(sf.units[v]["n"] // P):
                        m = pe.transpose(a[:, t * P:(t + 1) * P], soft_w[:, v % 2, t * P:(t + 1) * P], ident[:])
                    m.then_inc(S(p + "turn"), 1)
                if u >= 2:
                    v = u - 2
                    pe.wait_ge(S(p + "turned"), v + 1)
                    if v in out_waits:
                        pe.wait_ge(S(p + "o_out"), out_waits[v])
                    m = sf.units[v]["pv"](pe, soft_t[:, v % 2, :])
                    m.then_inc(S(p + "pv"), 1)

        def soft_dve(dve, st, sf, between):
            U = len(sf.units)
            p = sf.p
            for u in range(U + 2):
                if u < U:
                    n, mask = sf.units[u]["n"], sf.units[u]["mask"]
                    dve.wait_ge(S(p + "scores"), u + 1)
                    if u >= 2:
                        dve.wait_ge(S(p + "turn"), u - 1)
                    if mask is None:
                        st.then(dve.tensor_reduce(soft_m[:, u % 2, 0:1], sf.area(u, n), AX, ALU.max))
                    else:
                        st.then(dve.tensor_tensor_reduce(soft_w[:, u % 2, 0:n], sf.area(u, n), mask, 1.0, -3e38,
                                                         ALU.add, ALU.max, soft_m[:, u % 2, 0:1]))
                    dve.tensor_scalar(soft_m[:, u % 2, 1:2], soft_m[:, u % 2, 0:1], -sf.scale, None, ALU.mult)\
                       .then_inc(S(p + "max"), 1)
                if 1 <= u <= U:
                    v = u - 1
                    n = sf.units[v]["n"]
                    dve.wait_ge(S(p + "exp"), v + 1)
                    st.then(dve.reciprocal(soft_m[:, v % 2, 3:4], soft_m[:, v % 2, 2:3]))
                    dve.tensor_scalar(soft_w[:, v % 2, 0:n], soft_w[:, v % 2, 0:n], soft_m[:, v % 2, 3:4], None,
                                      ALU.mult).then_inc(S(p + "weights"), 1)
                between(u)

        def soft_act(act, sf, evacs, between):
            U = len(sf.units)
            p = sf.p
            for u in range(U + 2):
                if u < U:
                    n, mask = sf.units[u]["n"], sf.units[u]["mask"]
                    act.wait_ge(S(p + "max"), u + 1)
                    src = sf.area(u, n) if mask is None else soft_w[:, u % 2, 0:n]
                    act.activation(soft_w[:, u % 2, 0:n], src, ACT.Exp, scale=sf.scale, bias=soft_m[:, u % 2, 1:2],
                                   accum_out=soft_m[:, u % 2, 2:3]).then_inc(S(p + "exp"), 1)
                between(u)
                if 1 <= u <= U:
                    v = u - 1
                    n = sf.units[v]["n"]
                    act.wait_ge(S(p + "turn"), v + 1)
                    if v >= 2:
                        act.wait_ge(S(p + "pv"), v - 1)
                    act.activation(soft_t[:, v % 2, 0:n], sf.area(v, n), ACT.Copy).then_inc(S(p + "turned"), 1)
                if u >= 2 and (u - 2) in evacs:
                    act.wait_ge(S(p + "pv"), u - 1)
                    dst, src = evacs[u - 2]
                    act.activation(dst, src, ACT.Copy).then_inc(S(p + "o_out"), 1)

        def ffn_act_all(act, p, c0, ready):
            norm_act(act, p, xT, ready)
            ffn_act(act, p, c0)

        def ffn_dve_all(dve, p, c0, gain, ready):
            scaled_dve(dve, p, hT, xT, gain, False, ready)
            norm_dve(dve, p)
            ffn_dve(dve, p, c0)

        def halves(ap, m):
            v = ap.rearrange("p a t -> p (a t)").rearrange("p (b h m) -> p b h m", h=2, m=m)
            return v[:, :, 0, :], v[:, :, 1, :]

        def last_of(first, m):
            return first[:, :, m - 1:m].broadcast_to([P, first.shape[1], m])

        def apply_scores(pe, b, h, v, a):
            po, ct = 64 * (h % 2), h // 2
            o = bank2(b)[po:po + 64, ct, :]
            pe.matmul(o, v[:, 0, 64 * h:64 * h + 64], a[:, 0:T], start=True, stop=False, skip_group_check=True)
            return pe.matmul(o[:, P:T], v[:, 1, 64 * h:64 * h + 64], a[:, T:T + P], start=False, stop=True,
                             skip_group_check=True)

        def head_norm(dve, st, root, src, ors, gain, tile, gate):
            dve.wait_ge(S(root), 1)
            st.then(dve.reciprocal(ors, ors))
            for c in range(2):
                m = dve.scalar_tensor_tensor(mix[:, tile + c, :], src[:, c, :], pcol[:, gain + c:gain + c + 1],
                                             ors[:, c, :], ALU.mult, ALU.mult)
                if gate is not None:
                    st.then(m)
                    m = dve.tensor_tensor(mix[:, tile + c, :], mix[:, tile + c, :], gate[:, c, :], ALU.mult)
            m.then_inc(S("mix_done"), 1)

        with nc.Block() as block:
            xin = hT[:].rearrange("p k t -> p (k t)").rearrange("p (a n) -> p a n", a=TT)
            rows_in = sq[:, 0:2, :].rearrange("p a t -> p (a t)").rearrange("p (l n) -> p l n", l=4)

            def rows_dma(eng, l):
                for name, n in ROWS1:
                    r = rows_in[COL1[name]:COL1[name] + n, l, :]
                    src = A[name][l]
                    if name in ("fox_q_norm", "fox_k_norm"):
                        for c in range(2):
                            eng.dma_start(r[:, 64 * c:64 * c + 64], src.rearrange("(a n) -> a n", a=1))\
                               .then_inc(S("rows"), 16)
                    elif name.endswith("conv_w"):
                        eng.dma_start(r, src.rearrange("j (k p) -> (j k) p", p=P)).then_inc(S("rows"), 16)
                    else:
                        eng.dma_start(r, src.rearrange("(k p) -> k p", p=P)).then_inc(S("rows"), 16)
                for name, n in ROWS2:
                    eng.dma_start(rows_in[COL2[name]:COL2[name] + n, 2 + l, :],
                                  A[name][l].rearrange("(k p) -> k p", p=P)).then_inc(S("rows"), 16)

            @block.sync
            def _(sp):
                sp.dma_start(xin, A["x"][0].rearrange("(a p) n -> p a n", p=P)).then_inc(S("x_in"), 16)
                rows_dma(sp, 1)
                load_ahead(sp, 1, 0)

            @block.scalar
            def _(act):
                rows_dma(act, 0)

            @block.gpsimd
            def _(pool):
                st = Step(pool, S("pool_step"))
                for m, v in ((ident, 0.0), (ones64, 0.0), (upper, 1.0), (neg_causal, 0.0), (ones, 1.0),
                             (zeros, 0.0), (epst, EPS)):
                    st.then(pool.memset(m[:], v))
                for c in range(2):
                    st.then(pool.memset(ones64[64 * c:64 * c + 64, 64 * c:64 * c + 64], 1.0))
                for c in (0, 2):
                    u = upper[:, c * P:(c + 1) * P]
                    st.then(pool.affine_select(out=u, in_=u, compare_op=ALU.is_ge, fill=0.0, base=0,
                                               pattern=[[1, P]], channel_multiplier=-1))
                u = neg_causal[:, P:2 * P]
                st.then(pool.affine_select(out=u, in_=u, compare_op=ALU.is_ge, fill=NEG, base=0, pattern=[[-1, P]],
                                           channel_multiplier=1))
                pool.affine_select(out=ident[:], in_=ident[:], compare_op=ALU.not_equal, fill=1.0, base=0,
                                   pattern=[[-1, P]], channel_multiplier=1).then_inc(S("masks"), 1)

            @block.tensor
            def _(pe):
                pe.wait_ge(S("masks"), 1)
                pe.wait_ge(S("x_in"), 16)
                for k in range(KD):
                    for a in range(TT):
                        m = pe.transpose(bank2(k // 2)[:, k % 2, a * P:(a + 1) * P], xin[:, a, k * P:(k + 1) * P],
                                         ident[:])
                    m.then_inc(S("x_turn"), 1)
                pe.wait_ge(S("rows"), 16 * 2 * (len(ROWS1) + 2 + len(ROWS2)))
                for l in range(DEPTH):
                    pe.transpose(PS[:, 4, l * NROW1:(l + 1) * NROW1], rows_in[0:NROW1, l, :], ident[0:NROW1, 0:NROW1])
                    m = pe.transpose(PS[:, 5, l * NROW2:(l + 1) * NROW2], rows_in[0:NROW2, 2 + l, :],
                                     ident[0:NROW2, 0:NROW2])
                m.then_inc(S("cols_turn"), 1)

            @block.vector
            def _(dve):
                for j in range(4):
                    dve.wait_ge(S("x_turn"), 2 * j + 2)
                    dve.tensor_copy(xT[:, 2 * j:2 * j + 2, :], bank2(j)).then_inc(S("x_out"), 1)
                dve.wait_ge(S("cols_turn"), 1)
                dve.tensor_copy(cols1[:], bank(4, 2 * NROW1).rearrange("p (l n) -> p l n", l=2))
                dve.tensor_copy(cols2[:], bank(5, 2 * NROW2).rearrange("p (l n) -> p l n", l=2))

        clear_signals()
        end_part()

        take = carve()
        gq, gk, gg, fq, fk, sz, db, dc, dv = (take(2, T) for _ in range(9))
        gv, fv = take(2, T), take(2, T)
        PAD = 4
        xp, Bp, Cp, cp = (take(2, PAD + T) for _ in range(4))
        xs, Bc, Cc, cc = (take(2, T) for _ in range(4))
        mix = take(KD, T)
        hU = mix
        wsm = take(KD, 24)
        wgu = take(T)
        lr = take(T)
        zg, za = take(2, T), take(2, T)
        Ef, Eg = take(2, T), take(2, T)
        Kd, Qd = take(2, T), take(2, T)
        K64 = take(2, 2, 64)
        K128, Q128 = take(2, P), take(2, P)
        tb = take(2, 8)
        tA, tD = take(4), take(4)
        dcol = take(2)
        tz, te, ta = take(2, 8), take(2, 8), take(2, 8)
        acs = take(2, 4)
        bcs = take(2, 8, P)
        at_ = take(2, 3 * P)
        Gm = take(2, 3 * P)
        Lm = take(2, 3 * P)
        xd = take(2, T)
        (s_o, s_q, s_r), (g_o, g_q, g_r), (c_q, c_r), (f_o, f_q, f_r) = (
            [take(2, T) for _ in range(n)] for n in (3, 3, 2, 3))
        Fq, Fk = take(2, T), take(2, T)
        with nc.Fori(0, DEPTH) as layer:
            W = {n: A[n][layer] for n in ("ffn1_w_gate", "ffn1_w_up", "ffn1_w_down", "ffn2_w_gate", "ffn2_w_up",
                                          "ffn2_w_down", "w_in", "w_out", "gla_w_gate_up")}
            c_ffn1, c_proj = 0, 3 * NF
            c_out = c_proj + len(PROJ1)
            c_ffn2 = c_out + 4
            fox_units = []
            for h in range(4):
                for t in range(2):
                    po, ct = 64 * (h % 2), h // 2

                    def score(pe, a, h=h, t=t, po=po, ct=ct):
                        n = P * (t + 1)
                        pe.matmul(a[:, 0:n], fq[po:po + 64, ct, t * P:(t + 1) * P], fk[po:po + 64, ct, 0:n],
                                  start=True, stop=False, skip_group_check=True)
                        m = pe.matmul(a[:, 0:n], bcs[:, 0, h, :], upper[:, 0:n], start=False, stop=(t == 0),
                                      skip_group_check=True)
                        if t == 1:
                            m = pe.matmul(a[:, P:2 * P], bcs[:, 1, h, :], upper[:, 0:P], start=False, stop=True,
                                          skip_group_check=True)
                        return m

                    def pv(pe, w, h=h, t=t, po=po, ct=ct):
                        o = bank2(3)[po:po + 64, ct, t * P:(t + 1) * P]
                        for j in range(t + 1):
                            m = pe.matmul(o, fv[:, j, 64 * h:64 * h + 64], w[:, j * P:(j + 1) * P],
                                          start=(j == 0), stop=(j == t), skip_group_check=True)
                        return m
                    fox_units.append({"n": P * (t + 1), "mask": neg_causal[:, P * (1 - t):2 * P],
                                      "score": score, "pv": pv})
            fox = Soft("fox_", fox_units, 1.0)

            with nc.Block() as block:
                @block.sync
                def _(sp):
                    ffn_sp(sp, c_ffn1, W["ffn1_w_gate"], W["ffn1_w_up"], W["ffn1_w_down"])
                    gemm_sp(sp, c_proj, colchunks(W["w_in"], [o for _, o, _ in PROJ1]))
                    gemm_sp(sp, c_out, colchunks(W["w_out"], [CW * c for c in range(4)]))
                    ffn_sp(sp, c_ffn2, W["ffn2_w_gate"], W["ffn2_w_up"], W["ffn2_w_down"])
                    load_ahead(sp, 1, 1 - layer, c_ffn2 + 3 * NF)

                @block.gpsimd
                def _(pool):
                    pool.memset(at_, 0.0).then_inc(S("pool_zero"), 1)
                    for a in (xp, Bp, Cp, cp):
                        pool.memset(a[:, :, 0:PAD], 0.0).then_inc(S("pool_zero"), 1)

                @block.tensor
                def _(pe):
                    pe.sem_inc(S("chunk_done"), RING)
                    ffn_pe(pe, "ffn1_", c_ffn1, 1, layer)
                    gemm_pe1(pe, c_proj, 0, hU, "F", ready=S("mixu_in_ready"))
                    norm_pe(pe, "mix_")
                    gemm_pe1(pe, c_proj + 1, 1, hU, "F")
                    pe.wait_ge(S("small"), 16 * 10)
                    for k in range(KD):
                        pe.wait_ge(S("mix_in_ready"), k + 1)
                        m = pe.matmul(PS[0:16, 5, 0:T], wsm[:, k, 0:16], hT[:, k, :], start=(k == 0),
                                      stop=(k == KD - 1))
                    m.then_inc(S("lr_psum"), 1)
                    for t in range(2):
                        for k in range(KD):
                            m = pe.matmul(PS[:, 6, 8 * t:8 * t + 8], hT[:, k, t * P:(t + 1) * P], wsm[:, k, 16:24],
                                          start=(k == 0), stop=(k == KD - 1))
                    m.then_inc(S("tok_psum"), 1)
                    def proj(n0, n1):
                        for n in range(n0, n1):
                            if n >= 2:
                                pe.wait_ge(S("proj_out"), n - 1)
                            gemm_pe1(pe, c_proj + n, n % 2, hT, PROJ1[n][2])

                    def ssd_row(h):
                        b = 5 + 2 * (h % 2)
                        if h >= 2:
                            pe.wait_ge(S("seg"), h - 1)
                        pe.matmul(PS[:, b, 0:T], bcs[:, 0, 4 + h, :], upper[:, 0:T], start=True, stop=False,
                                  skip_group_check=True)
                        pe.matmul(PS[:, b, P:T], bcs[:, 1, 4 + h, :], upper[:, 0:P], start=False, stop=True,
                                  skip_group_check=True).then_inc(S("acs_row"), 1)

                    def ssd_pv(h):
                        pe.wait_ge(S("ssd_w"), h + 1)
                        apply_scores(pe, 3, h, xd, Lm[:, h % 2, :]).then_inc(S("ssd_pv"), 1)

                    def gla_maps(h):
                        po, ct, b = 64 * (h % 2), h // 2, 4 + h % 2
                        if h >= 2:
                            pe.wait_ge(S("gla_w"), h - 1)
                        hp = slice(po, po + 64)
                        for t in range(2):
                            o = t * P
                            c = 2 * t * P
                            pe.matmul(PS[0:64, b, c:c + 64], Kd[hp, ct, o:o + 64], Qd[hp, ct, o:o + 64],
                                      start=True, stop=True, skip_group_check=True)
                            pe.matmul(PS[0:64, b, c + 64:c + P], K64[hp, ct, t, :], Qd[hp, ct, o + 64:o + P],
                                      start=True, stop=True, skip_group_check=True)
                            pe.matmul(PS[64:128, b, c + 64:c + P], Kd[hp, ct, o + 64:o + P],
                                      Qd[hp, ct, o + 64:o + P], start=True, stop=True, skip_group_check=True)
                        pe.matmul(PS[:, b, P:2 * P], K128[hp, ct, :], Q128[hp, ct, :], start=True, stop=True,
                                  skip_group_check=True).then_inc(S("gla_maps"), 1)

                    def gla_pv(h):
                        pe.wait_ge(S("gla_w"), h + 1)
                        apply_scores(pe, 2, h, gv, at_[:, h % 2, :]).then_inc(S("gla_pv"), 1)

                    proj(2, 3)
                    pe.wait_ge(S("lr"), 1)
                    for c in range(2):
                        m = pe.matmul(bank2(7)[:, c, :], wgu[0:16, c * P:(c + 1) * P], lr[0:16, :], start=True,
                                      stop=True)
                    m.then_inc(S("gate_psum"), 1)
                    proj(3, 4)
                    pe.wait_ge(S("tok_vals"), 1)
                    pe.matmul(PS[:, 6, 32:36], upper[:, 0:P], ta[:, 0, 4:8], start=True, stop=True)
                    pe.matmul(PS[:, 6, 36:40], ones[:], ta[:, 0, 4:8], start=True, stop=False)
                    pe.matmul(PS[:, 6, 36:40], upper[:, 0:P], ta[:, 1, 4:8], start=False, stop=True)\
                      .then_inc(S("acs_psum"), 1)
                    proj(4, 6)
                    pe.wait_ge(S("conv_out"), 6)
                    for c in range(2):
                        for t in range(2):
                            m = pe.transpose(bank2(2)[:, t, c * P:(c + 1) * P], xs[:, c, t * P:(t + 1) * P], ident[:])
                    m.then_inc(S("xs_turn"), 1)
                    for g in range(2):
                        pe.matmul(PS[:, 3 + g, 0:T], Bc[:, g, 0:P], Cc[:, g, :], start=True, stop=True)
                        pe.matmul(PS[:, 3 + g, T:T + P], Bc[:, g, P:T], Cc[:, g, P:T], start=True, stop=True)\
                          .then_inc(S("cb_psum"), 1)
                    proj(6, 7)
                    pe.wait_ge(S("bcs"), 16)
                    ssd_row(0)
                    ssd_row(1)
                    proj(7, 8)
                    pe.wait_ge(S("xd"), 1)
                    ssd_pv(0)
                    ssd_row(2)
                    ssd_pv(1)
                    ssd_row(3)
                    proj(8, 9)
                    ssd_pv(2)
                    ssd_pv(3)
                    pe.wait_ge(S("gla_ops"), 1)
                    gla_maps(0)
                    gla_maps(1)
                    pe.wait_ge(S("fox_qk_sq"), 2)
                    for c in range(2):
                        pe.matmul(bank(6 + c), ones64[:], (Fq, Fk)[c], start=True, stop=True)\
                          .then_inc(S("fox_qk_sum"), 1)
                    proj(9, 10)
                    gla_pv(0)
                    gla_maps(2)
                    gla_pv(1)
                    gla_maps(3)
                    proj(10, 11)
                    gla_pv(2)
                    gla_pv(3)
                    pe.wait_ge(S("ssd_sq"), 1)
                    pe.matmul(bank(3), ones[:], s_q, start=True, stop=True).then_inc(S("ssd_sum"), 1)
                    proj(11, 12)
                    pe.wait_ge(S("gla_sq"), 1)
                    pe.matmul(bank(2), ones64[:], g_q, start=True, stop=True).then_inc(S("gla_sum"), 1)
                    pe.wait_ge(S("fox_qk"), 2)
                    pe.wait_ge(S("ssd_root"), 1)

                    def between(u):
                        if u < 2:
                            proj(12 + u, 13 + u)
                        if u == 4:
                            pe.wait_ge(S("sc_sq"), 1)
                            pe.wait_ge(S("gla_root"), 1)
                            pe.matmul(bank(2), ones64[:], c_q, start=True, stop=True).then_inc(S("sc_sum"), 1)
                    soft_pe(pe, fox, {}, between)
                    pe.wait_ge(S("fox_sq"), 1)
                    pe.matmul(bank(4), ones64[:], f_q, start=True, stop=True).then_inc(S("fox_sum"), 1)
                    for last in range(2):
                        pe.wait_ge(S("mix_done"), (3, 4)[last])
                        for n in range(4):
                            if not last:
                                wait_chunk(pe, c_out + n)
                            w = chunk(c_out + n, KD, CW)
                            for f in range(2):
                                for k in ((0, 1, 4, 5, 6, 7), (2, 3))[last]:
                                    if n == 3 and f == 0 and k == 0:
                                        pe.wait_ge(S("fox_o_out"), 1)
                                    m = pe.matmul(bank2(n)[:, f, :], w[:, k, f * P:(f + 1) * P], mix[:, k, :],
                                                  start=(f == 0 and k == 0), stop=(k == 3), skip_group_check=True)
                            if last:
                                m.then_inc(S("chunk_done"), 1)
                    ffn_pe(pe, "ffn2_", c_ffn2, 1, layer)

                @block.scalar
                def _(act):
                    st = Step(act, S("act_step"))
                    for o, n, at in ((A_LR, 16, 0), (B_F, 4, 16), (C_DT, 4, 20)):
                        act.dma_start(wsm[:, :, at:at + n], W["w_in"][:, o:o + n]
                                       .rearrange("(k p) f -> p k f", p=P)).then_inc(S("small"), 16)
                    act.dma_start(wgu[0:16, :], W["gla_w_gate_up"]).then_inc(S("small"), 16)
                    for t in range(2):
                        for name, at in (("fox_b_forget", 0), ("ssm_dt_bias", 4)):
                            act.dma_start(tb[:, t, at:at + 4], A[name][layer].partition_broadcast(P))\
                                .then_inc(S("small"), 16)
                    act.dma_start(tD, A["ssm_D"][layer].partition_broadcast(P)).then_inc(S("small"), 16)
                    act.dma_start(tA, A["ssm_A_log"][layer].partition_broadcast(P)).then_inc(S("small"), 16)
                    ffn_act_all(act, "ffn1_", c_ffn1, None)
                    norm_act(act, "mix_", xT, S("ffn1_x_ready"))
                    pads = {"xs": xp, "B": Bp, "C": Cp}
                    dst = {"a_q": gq, "a_k": gk, "a_v": gv, "b_q": fq, "b_k": fk, "b_v": fv, "d_c": dc, "d_v": dv,
                           "d_b": db, "a_g": gg, "c_z": sz}

                    def out_of_bank(n0, n1):
                        for n in range(n0, n1):
                            name = PROJ1[n][0]
                            act.wait_ge(S("chunk_done"), RING + c_proj + n + 1)
                            o = pads[name][:, :, PAD:PAD + T] if name in pads else dst[name]
                            f = ACT.Silu if name in ("a_g", "c_z") else ACT.Copy
                            if n < EARLY:
                                act.wait_ge(S("early_out"), n + 1)
                            act.activation(o, o if n < EARLY else bank2(n % 2), f, scale=(0.125 if name == "a_q" else 1.0))\
                               .then_inc(S("proj_out"), 1)

                    def decay(h):
                        act.wait_ge(S("seg"), h + 1)
                        act.activation(Lm[:, h % 2, :], Lm[:, h % 2, :], ACT.Exp).then_inc(S("seg_exp"), 1)

                    def gla_cross(h):
                        act.wait_ge(S("gla_maps"), h + 1)
                        if h >= 2:
                            act.wait_ge(S("gla_pv"), h - 1)
                        act.activation(at_[:, h % 2, P:2 * P], PS[:, 4 + h % 2, P:2 * P], ACT.Copy)\
                           .then_inc(S("gla_cross"), 1)

                    def root(name, b, dst, n):
                        act.wait_ge(S(name + "_sum"), 1)
                        act.activation(dst, bank2(b), ACT.Sqrt, scale=1.0 / n, bias=epst[:, 0:1])\
                           .then_inc(S(name + "_root"), 1)

                    act.wait_ge(S("pool_zero"), 5)
                    out_of_bank(0, 2)
                    act.wait_ge(S("lr_psum"), 1)
                    act.activation(lr[0:16, :], PS[0:16, 5, 0:T], ACT.Copy).then_inc(S("lr"), 1)
                    act.wait_ge(S("tok_z"), 1)
                    st.then(act.activation(te, tz, ACT.Abs))
                    st.then(act.activation(te, te, ACT.Exp, scale=-1.0))
                    act.activation(te, te, ACT.Ln, bias=1.0).then_inc(S("tok_ln"), 1)
                    act.wait_ge(S("small"), 16 * 10)
                    act.activation(tA, tA, ACT.Exp).then_inc(S("A_exp"), 1)
                    act.wait_ge(S("gate_psum"), 1)
                    for c in range(2):
                        g = act.activation(zg[:, c, :], bank2(7)[:, c, :], ACT.Identity,
                                           bias=pcol[:, COL1["gla_b_gate"] + c:COL1["gla_b_gate"] + c + 1])
                    g.then_inc(S("gate_z"), 1)
                    act.wait_ge(S("gate_z"), 1)
                    st.then(act.activation(Ef, zg, ACT.Abs))
                    st.then(act.activation(Ef, Ef, ACT.Exp, scale=-1.0))
                    act.activation(Ef, Ef, ACT.Ln, bias=1.0).then_inc(S("gate_ln"), 1)
                    out_of_bank(2, 3)
                    act.wait_ge(S("gla_pref"), 1)
                    act.activation(Ef, za, ACT.Exp)
                    act.activation(Eg, za, ACT.Exp, scale=-1.0)
                    act.activation(K64, K64, ACT.Exp).then_inc(S("gla_exp"), 1)
                    out_of_bank(3, 4)
                    for c in range(6):
                        act.wait_ge(S("conv_acc"), c + 1)
                        a = (xs, Bc, Cc)[c // 2][:, c % 2, :]
                        act.activation(a, a, ACT.Silu, bias=pcol[:, COL1["ssm_conv_b"] + c:COL1["ssm_conv_b"] + c + 1])\
                           .then_inc(S("conv_out"), 1)
                    out_of_bank(4, 5)
                    act.wait_ge(S("gla_pref"), 2)
                    act.activation(Q128, za[:, :, P:T], ACT.Exp)
                    act.activation(K128, K128, ACT.Exp).then_inc(S("gla_exp"), 1)
                    out_of_bank(5, 7)
                    act.wait_ge(S("proj_out"), 7)
                    act.activation(Fq, fq, ACT.Square).then_inc(S("fox_qk_sq"), 1)
                    decay(0)
                    decay(1)
                    out_of_bank(7, 8)
                    act.wait_ge(S("proj_out"), 8)
                    act.activation(Fk, fk, ACT.Square).then_inc(S("fox_qk_sq"), 1)
                    decay(2)
                    decay(3)
                    out_of_bank(8, 9)
                    gla_cross(0)
                    gla_cross(1)
                    act.wait_ge(S("fox_qk_sum"), 2)
                    for c in range(2):
                        act.activation((Fq, Fk)[c], bank2(6 + c), ACT.Sqrt, scale=1.0 / 64, bias=epst[:, 0:1])\
                           .then_inc(S("fox_qk_root"), 1)
                    out_of_bank(9, 10)
                    act.wait_ge(S("ssd_y"), 1)
                    act.activation(s_q, s_o, ACT.Square).then_inc(S("ssd_sq"), 1)
                    gla_cross(2)
                    gla_cross(3)
                    out_of_bank(10, 11)
                    root("ssd", 3, s_r, P)
                    act.wait_ge(S("gla_pv"), 4)
                    st.then(act.activation(g_o, bank2(2), ACT.Copy))
                    act.activation(g_q, g_o, ACT.Square).then_inc(S("gla_sq"), 1)
                    out_of_bank(11, 12)
                    root("gla", 2, g_r, 64)

                    def between(u):
                        if u < 2:
                            out_of_bank(12 + u, 13 + u)
                        if u == 3:
                            act.wait_ge(S("sc_y"), 1)
                            act.activation(c_q, db, ACT.Square).then_inc(S("sc_sq"), 1)
                        if u == 5:
                            root("sc", 2, c_r, 64)
                    soft_act(act, fox, {7: (f_o, bank2(3))}, between)
                    act.wait_ge(S("fox_o_out"), 1)
                    act.activation(f_q, f_o, ACT.Square).then_inc(S("fox_sq"), 1)
                    root("fox", 4, f_r, 64)
                    ffn_act_all(act, "ffn2_", c_ffn2, S("mixo_x_ready"))

                @block.vector
                def _(dve):
                    st = Step(dve, S("dve_step"))
                    dve.tensor_copy(pcol[:, 0:NROW1].unsqueeze(1), cols1[:, bass.ds(layer, 1), :])\
                       .then_inc(S("cols"), 1)
                    dve.wait_ge(S("cols"), 1)
                    ffn_dve_all(dve, "ffn1_", c_ffn1, COL1["ffn1_norm"], None)
                    scaled_dve(dve, "mixu_", hU, xT, COL1["mix_norm"], False, S("ffn1_x_ready"))
                    norm_dve(dve, "mix_")
                    scaled_dve(dve, "mix_", hT, xT, COL1["mix_norm"], True)
                    dve.wait_ge(S("pool_zero"), 5)
                    early_out_dve(dve, c_proj, (gq, xp[:, :, PAD:PAD + T]))
                    dve.wait_ge(S("tok_psum"), 1)
                    dve.wait_ge(S("small"), 16 * 10)
                    st.then(dve.tensor_tensor(tz, PS[:, 6, 0:16].rearrange("p (t n) -> p t n", t=2), tb, ALU.add))
                    st.then(dve.tensor_scalar(tz[:, :, 0:4], tz[:, :, 0:4], -1.0, None, ALU.mult))
                    dve.tensor_copy(ta, tz).then_inc(S("tok_z"), 1)
                    dve.tensor_copy(dcol[0:64, :], tD[0:64, :].rearrange("p (c h) -> p h c", h=2)[:, 0, :])
                    st.then(dve.tensor_copy(dcol[64:128, :],
                                            tD[64:128, :].rearrange("p (c h) -> p h c", h=2)[:, 1, :]))
                    dve.wait_ge(S("tok_ln"), 1)
                    dve.wait_ge(S("A_exp"), 1)
                    st.then(dve.tensor_scalar(ta, ta, 0.0, None, ALU.max))
                    st.then(dve.tensor_tensor(ta, ta, te, ALU.add))
                    st.then(dve.tensor_copy(te, ta))
                    st.then(dve.tensor_tensor(ta[:, :, 4:8], ta[:, :, 4:8], over(tA, 2), ALU.mult))
                    dve.tensor_scalar(ta[:, :, 4:8], ta[:, :, 4:8], -1.0, None, ALU.mult).then_inc(S("tok_vals"), 1)
                    dve.wait_ge(S("tok_vals"), 1)
                    for t in range(2):
                        for h in range(8):
                            dve.tensor_scalar(bcs[:, t, h, :], ones[:], ta[:, t, h:h + 1], None, ALU.mult)\
                               .then_inc(S("bcs"), 1)
                    dve.wait_ge(S("gate_ln"), 1)
                    st.then(dve.tensor_scalar(za, zg, 0.0, None, ALU.min))
                    st.then(dve.tensor_tensor(za, za, Ef, ALU.subtract))
                    st.then(dve.tensor_scalar(za, za, 1.0 / 16.0, None, ALU.mult))
                    for m in (1, 2, 4, 8, 16, 32):
                        first, second = halves(za, m)
                        st.then(dve.tensor_tensor(second, second, last_of(first, m), ALU.add))
                    first, second = halves(za, 64)
                    k64 = K64.rearrange("p a b n -> p (a b) n")
                    dve.tensor_tensor(k64, last_of(first, 64), first, ALU.subtract).then_inc(S("gla_pref"), 1)

                    def conv(c):
                        src = (xp, Bp, Cp)[c // 2][:, c % 2, :]
                        dst = (xs, Bc, Cc)[c // 2][:, c % 2, :]
                        dve.wait_ge(S("proj_out"), 2 + c // 2)
                        w0 = COL1["ssm_conv_w"] + c
                        st.then(dve.tensor_scalar(dst, src[:, PAD:PAD + T], pcol[:, w0 + 18:w0 + 19], None, ALU.mult))
                        for j in range(3):
                            m = dve.scalar_tensor_tensor(dst, src[:, PAD - 3 + j:PAD - 3 + j + T],
                                                         pcol[:, w0 + 6 * j:w0 + 6 * j + 1], dst, ALU.mult, ALU.add)
                            if j < 2:
                                st.then(m)
                        m.then_inc(S("conv_acc"), 1)

                    for c in range(4):
                        conv(c)
                    dve.wait_ge(S("gla_exp"), 1)
                    st.then(dve.tensor_tensor(second, second, last_of(first, 64), ALU.add))
                    dve.tensor_tensor(K128, za[:, :, P - 1:P].broadcast_to([P, 2, P]), za[:, :, 0:P], ALU.subtract)\
                       .then_inc(S("gla_pref"), 1)
                    conv(4)
                    conv(5)
                    dve.wait_ge(S("acs_psum"), 1)
                    st.then(dve.tensor_copy(acs, PS[:, 6, 32:40].rearrange("p (t n) -> p t n", t=2)))
                    dve.wait_ge(S("proj_out"), 5)
                    dve.wait_ge(S("gla_exp"), 2)
                    st.link(dve.tensor_tensor(Kd, gk, Eg, ALU.mult))
                    st.link(dve.tensor_tensor(Qd, gq, Ef, ALU.mult))
                    st.link(dve.tensor_tensor(k64, halves(gk, 64)[0], k64, ALU.mult))
                    st.link(dve.tensor_tensor(K128, gk[:, :, 0:P], K128, ALU.mult))
                    dve.tensor_tensor(Q128, gq[:, :, P:T], Q128, ALU.mult).then_inc(S("gla_ops"), 1)
                    dve.wait_ge(S("xs_turn"), 1)
                    dve.tensor_tensor(xd.rearrange("p t (h n) -> p t h n", h=4),
                                      bank2(2).rearrange("p t (h n) -> p t h n", h=4),
                                      te[:, :, 4:8].unsqueeze(3).broadcast_to([P, 2, 4, 64]), ALU.mult)\
                       .then_inc(S("xd"), 1)
                    for g in range(2):
                        dve.wait_ge(S("cb_psum"), g + 1)
                        dve.tensor_tensor(Gm[:, g, :], PS[:, 3 + g, 0:3 * P], upper[:], ALU.mult)\
                           .then_inc(S("cb_masked"), 1)
                    for h in range(5):
                        if h < 4:
                            dve.wait_ge(S("acs_row"), h + 1)
                            if h >= 2:
                                dve.wait_ge(S("ssd_pv"), h - 1)
                            b = 5 + 2 * (h % 2)
                            dve.tensor_scalar(Lm[:, h % 2, 0:T], PS[:, b, 0:T], acs[:, 0, h:h + 1], 0.0,
                                              ALU.subtract, ALU.min)
                            dve.tensor_scalar(Lm[:, h % 2, T:T + P], PS[:, b, P:T], acs[:, 1, h:h + 1], 0.0,
                                              ALU.subtract, ALU.min).then_inc(S("seg"), 1)
                        if h >= 1:
                            g = h - 1
                            dve.wait_ge(S("seg_exp"), g + 1)
                            dve.wait_ge(S("cb_masked"), 2)
                            dve.tensor_tensor(Lm[:, g % 2, :], Lm[:, g % 2, :], Gm[:, g // 2, :], ALU.mult)\
                               .then_inc(S("ssd_w"), 1)

                    def gla_masked(h):
                        dve.wait_ge(S("gla_cross"), h + 1)
                        if h >= 2:
                            dve.wait_ge(S("gla_pv"), h - 1)
                        b = 4 + h % 2
                        for t in range(2):
                            c = 2 * t * P
                            dve.tensor_tensor(at_[0:64, h % 2, c:c + 64], PS[0:64, b, c:c + 64], upper[0:64, 0:64],
                                              ALU.mult)
                            dve.tensor_copy(at_[0:64, h % 2, c + 64:c + P], PS[0:64, b, c + 64:c + P])
                            m = dve.tensor_tensor(at_[64:128, h % 2, c + 64:c + P], PS[64:128, b, c + 64:c + P],
                                                  upper[64:128, 64:128], ALU.mult)
                        m.then_inc(S("gla_w"), 1)
                    gla_masked(0)
                    gla_masked(1)
                    dve.wait_ge(S("fox_qk_root"), 2)
                    for c, (a, r, g) in enumerate(((fq, Fq, "fox_q_norm"), (fk, Fk, "fox_k_norm"))):
                        st.then(dve.reciprocal(r, r))
                        m = dve.scalar_tensor_tensor(a, a, pcol[:, COL1[g]:COL1[g] + 1], r, ALU.mult, ALU.mult)
                        if c == 0:
                            st.then(m)
                            m = dve.tensor_scalar(a, a, 0.125, None, ALU.mult)
                        m.then_inc(S("fox_qk"), 1)
                    dve.wait_ge(S("ssd_pv"), 4)
                    for c in range(2):
                        st.then(dve.scalar_tensor_tensor(s_o[:, c, :], xs[:, c, :], dcol[:, c:c + 1],
                                                         bank2(3)[:, c, :], ALU.mult, ALU.add))
                    dve.wait_ge(S("proj_out"), 10)
                    dve.tensor_tensor(s_o, s_o, sz, ALU.mult).then_inc(S("ssd_y"), 1)
                    gla_masked(2)
                    gla_masked(3)
                    head_norm(dve, st, "ssd_root", s_o, s_r, COL1["ssm_norm"], 4, None)

                    def between(u):
                        if u == 1:
                            head_norm(dve, st, "gla_root", g_o, g_r, COL1["gla_norm"], 0, gg)
                        if u == 2:
                            dve.wait_ge(S("proj_out"), 14)
                            dve.wait_ge(S("pool_zero"), 5)
                            st.then(dve.tensor_tensor(cp[:, :, PAD:PAD + T], dc, dv, ALU.mult))
                            for c in range(2):
                                w0 = COL1["sc_conv_w"] + c
                                st.then(dve.tensor_scalar(cc[:, c, :], cp[:, c, PAD:PAD + T], pcol[:, w0 + 4:w0 + 5],
                                                          None, ALU.mult))
                                for j in range(2):
                                    st.then(dve.scalar_tensor_tensor(cc[:, c, :], cp[:, c, PAD - 2 + j:PAD - 2 + j + T],
                                                                     pcol[:, w0 + 2 * j:w0 + 2 * j + 1],
                                                                     cc[:, c, :], ALU.mult, ALU.add))
                            dve.tensor_tensor(db, db, cc, ALU.mult).then_inc(S("sc_y"), 1)
                        if u == 6:
                            head_norm(dve, st, "sc_root", db, c_r, COL1["sc_out_norm"], 6, None)
                    soft_dve(dve, st, fox, between)
                    head_norm(dve, st, "fox_root", f_o, f_r, COL1["fox_out_norm"], 2, None)
                    residual_dve(dve, "mixo_", c_out)
                    ffn_dve_all(dve, "ffn2_", c_ffn2, COL1["ffn2_norm"], S("mixo_x_ready"))

            clear_signals()
        end_part()

        take = carve()
        memT = take(KD, T)
        rmem = take(T)
        cosT, sinT = take(T), take(T)
        dmask1, dmask0 = take(3 * T), take(3 * P)
        lmask = take(7, 64)
        lb01, lbc = take(2, KD), take(2, KD)
        base = take.at[0]
        aq, ak = take(12, T), take(12, T)
        av = take(2, AW)
        hq, hk, hP = take(KD, T), take(KD, T), take(KD, T)
        hv = take(2, D)
        hog = take(KD, T)
        X = take(8, 2, T)
        hat, a128 = take(2, P), take(2, P)
        Xf = X.rearrange("p l h t -> p (l h t)")
        yat = Xf[:, 0:1024].rearrange("p (k t) -> p k t", k=4)
        xa, xb = (Xf[:, 2048 * i:2048 * (i + 1)].rearrange("p (k t) -> p k t", k=KD) for i in range(2))
        mt = work[:, 3072:3968].rearrange("p (b l n) -> p b l n", b=2, l=7)
        hU = aq[:, 0:KD, :]
        rp = sq[:].rearrange("p k t -> p (k t)").rearrange("p (b s f t) -> p b s f t", b=2, s=2, f=2)
        sgA, sgB = hP, hk
        mg = hv.rearrange("p t n -> p (t n)").rearrange("p (k t) -> p k t", k=KD)
        brt = hog[:, 0:2, :]
        take.at[0] = base
        memn, kx, qx, ox = (take(KD, T) for _ in range(4))
        vx = take(2, D)

        with nc.Block() as block:
            min_ = hT[:].rearrange("p k t -> p (k t)").rearrange("p (a n) -> p a n", a=TT)
            posi = work[:, 0:T].bitcast(I32)
            ang, nf, rr = work[:, T:2 * T], work[:, 2 * T:3 * T], work[:, 3 * T:4 * T]
            ni = work[:, 4 * T:5 * T].bitcast(I32)
            iot = work[:, 5 * T:6 * T].bitcast(I32)
            low = work[:, 6 * T:7 * T].bitcast(I32)
            invf = work[:, 7 * T:7 * T + 1]
            lbm = work[:, 8 * T:8 * T + 8]

            @block.sync
            def _(sp):
                sp.dma_start(min_, A["mem_2"][0].rearrange("(a p) n -> p a n", p=P)).then_inc(S("mem_in"), 16)
                sp.dma_start(posi, A["positions_2"][0].partition_broadcast(P)).then_inc(S("rope_in"), 16)
                sp.dma_start(invf, A["inv_freq"].rearrange("(p a) -> p a", a=1)).then_inc(S("rope_in"), 16)
                for l in range(DEPTH):
                    sp.dma_start(prow[8 * l:8 * l + 8, :], A["hgrn_lower_bounds_2"][l]
                                 .rearrange("(k p) -> k p", p=P)).then_inc(S("rows"), 16)
                for j in range(2):
                    sp.wait_ge(ahead[1][j], 16 * (DEPTH + 1))
                load_ahead(sp, 2, 0)

            @block.gpsimd
            def _(pool):
                st = Step(pool, S("pool_step"))
                pool.iota(iot, pattern=[[-1, T]], base=384, channel_multiplier=1).then_inc(S("iota"), 1)
                st.then(pool.memset(lmask, 0.0))
                for c in range(2):
                    q = slice(64 * c, 64 * c + 64)
                    st.then(pool.affine_select(out=lmask[q, 0, :], in_=lmask[q, 0, :], compare_op=ALU.not_equal,
                                               fill=1.0, base=0, pattern=[[-1, 64]], channel_multiplier=1))
                    for l in range(6):
                        m = 1 << l
                        v = lmask[q, l + 1, :].rearrange("p (b h m) -> p b h m", h=2, m=m)[:, :, 1, :]
                        st.then(pool.memset(v, 1.0))
                        st.then(pool.affine_select(out=v, in_=v, compare_op=ALU.is_ge, fill=0.0, base=0,
                                                   pattern=[[-2 * m, 32 // m], [0, m]], channel_multiplier=1))
                        st.then(pool.affine_select(out=v, in_=v, compare_op=ALU.is_ge, fill=0.0, base=m - 1,
                                                   pattern=[[2 * m, 32 // m], [0, m]], channel_multiplier=-1))
                st.then(pool.memset(dmask1[:, 0:T], 0.0))
                pool.wait_ge(S("dil"), 2)
                d3 = dmask1.rearrange("p (g n) -> p g n", g=3)
                st.then(pool.affine_select(out=d3, in_=d3, compare_op=ALU.is_ge, fill=NEG, base=P,
                                           pattern=[[0, 3], [-1, T]], channel_multiplier=1))
                st.then(pool.affine_select(out=dmask1[:, 0:T], in_=dmask1[:, 0:T], compare_op=ALU.is_ge, fill=NEG,
                                           base=0, pattern=[[1, T]], channel_multiplier=-1))
                pool.tensor_copy(dmask0.rearrange("p (g n) -> p g n", g=3), d3[:, :, P:T])\
                    .then_inc(S("dmasks"), 1)

            @block.tensor
            def _(pe):
                pe.wait_ge(S("mem_in"), 16)
                for k in range(KD):
                    for a in range(TT):
                        m = pe.transpose(bank2(k // 2)[:, k % 2, a * P:(a + 1) * P], min_[:, a, k * P:(k + 1) * P],
                                         ident[:])
                    m.then_inc(S("mem_turn"), 1)
                pe.wait_ge(S("rows"), 32)
                pe.transpose(bank(5, 16), prow[0:16, :], ident[0:16, 0:16]).then_inc(S("lb_turn"), 1)
                norm_pe(pe, "mem_")

            @block.scalar
            def _(act):
                norm_act(act, "mem_", memT, S("mem_out"))
                act.wait_ge(S("lb_z"), 1)
                act.activation(lb01, lb01, ACT.Exp).then_inc(S("lb_exp"), 1)
                act.wait_ge(S("angles"), 1)
                act.activation(sinT, rr, ACT.Sin).then_inc(S("tables"), 1)
                act.activation(cosT, nf, ACT.Sin).then_inc(S("tables"), 1)

            @block.vector
            def _(dve):
                st = Step(dve, S("dve_step"))
                dve.wait_ge(S("iota"), 1)
                for g, m in ((1, 3), (2, 15)):
                    st.then(dve.tensor_scalar(low, iot, m, None, ALU.bitwise_and))
                    st.then(dve.tensor_scalar(nf, low, 1.0, NEG, ALU.min, ALU.mult))
                    dve.tensor_copy(dmask1[:, g * T:(g + 1) * T], nf).then_inc(S("dil"), 1)
                    dve.wait_ge(S("dil"), g)
                for j in range(4):
                    dve.wait_ge(S("mem_turn"), 2 * j + 2)
                    dve.tensor_copy(memT[:, 2 * j:2 * j + 2, :], bank2(j)).then_inc(S("mem_out"), 1)
                norm_dve(dve, "mem_")
                st.then(dve.tensor_copy(rmem, rstd[:]))
                dve.wait_ge(S("lb_turn"), 1)
                st.then(dve.tensor_copy(lb01, bank(5, 16).rearrange("p (l k) -> p l k", l=2)))
                st.then(dve.tensor_tensor(lbm, lb01[:, 0, :], lb01[:, 1, :], ALU.max))
                dve.tensor_tensor(lb01, lb01, over(lbm, 2), ALU.subtract).then_inc(S("lb_z"), 1)
                dve.wait_ge(S("lb_exp"), 1)
                st.then(dve.tensor_tensor(lbm, lb01[:, 0, :], lb01[:, 1, :], ALU.add))
                st.then(dve.reciprocal(lbm, lbm))
                st.then(dve.tensor_tensor(lb01[:, 1, :], lb01[:, 1, :], lbm, ALU.mult))
                st.then(dve.memset(lb01[:, 0, :], 0.0))
                dve.wait_ge(S("rope_in"), 32)
                st.then(dve.tensor_copy(ang, posi))
                st.then(dve.tensor_scalar(ang, ang, invf, None, ALU.mult))
                st.then(dve.tensor_scalar(nf, ang, 1.0 / (2.0 * np.pi), None, ALU.mult))
                st.then(dve.tensor_copy(ni, nf))
                st.then(dve.tensor_copy(nf, ni))
                c1 = 6.28125
                c2 = float(np.float32(2.0 * np.pi - c1) - np.float32(2.0 * np.pi - c1) % np.float32(2.0 ** -20))
                for c in (c1, c2, 2.0 * np.pi - c1 - c2):
                    st.then(dve.scalar_tensor_tensor(ang, nf, -c, ang, ALU.mult, ALU.add))
                PI = 3.1415925
                st.then(dve.tensor_scalar(rr, ang, -PI, PI, ALU.max, ALU.min))
                st.then(dve.tensor_scalar(ang, rr, -1.0, None, ALU.mult))
                st.then(dve.tensor_tensor(nf, ang, rr, ALU.max))
                dve.tensor_scalar(nf, nf, -1.0, float(np.pi / 2), ALU.mult, ALU.add).then_inc(S("angles"), 1)

        clear_signals()
        end_part()

        with nc.Fori(0, DEPTH) as layer:
            W = {n: A[n + "_2"][layer] for n in ("ffn1_w_gu", "ffn1_w_down", "ffn2_w_gu", "ffn2_w_down", "w_in",
                                                 "w_att_branch", "w_hgrn_branch", "w_mix_out", "xattn_wq",
                                                 "xattn_wkv", "xattn_wo")}
            c_ffn1, c_proj = 0, 3 * NF
            c_gate = c_proj + len(PROJ2)
            c_hg = c_gate + len(GATES)
            c_att = c_hg + 4
            c_mix = c_att + 4
            c_cross = c_mix + 4
            c_xo = c_cross + len(CROSS)
            c_ffn2 = c_xo + 4
            idx = {(name, c): n for n, (name, _, _, c) in enumerate(PROJ2)}
            evens = [CW * c for c in range(4)]
            HG_SUMS = (6, 7, 2, 3)

            att_units = []
            for h in range(4):
                for t in range(2):
                    def score(pe, a, h=h, t=t):
                        w = P * (t + 1)
                        for g in range(3):
                            m = pe.matmul(a[:, g * w:(g + 1) * w], aq[:, 4 * g + h, t * P:(t + 1) * P],
                                          ak[:, 4 * g + h, 0:w], start=True, stop=True, skip_group_check=True)
                        return m

                    def pv(pe, w, h=h, t=t):
                        o = bank2(2 + h // 2)[:, h % 2, t * P:(t + 1) * P]
                        n = 3 * (t + 1)
                        for j in range(n):
                            g, kt = j // (t + 1), j % (t + 1)
                            m = pe.matmul(o, av[:, kt, (4 * g + h) * P:(4 * g + h + 1) * P],
                                          w[:, j * P:(j + 1) * P], start=(j == 0), stop=(j == n - 1),
                                          skip_group_check=True)
                        return m
                    att_units.append({"n": 3 * P * (t + 1), "mask": (dmask0, dmask1)[t], "score": score, "pv": pv})
            att = Soft("att_", att_units, float(P) ** -0.5)

            x_units = []
            for h in range(4):
                for t in range(2):
                    def score(pe, a, h=h, t=t):
                        pe.wait_ge(S("cross_out"), CROSS.index(("q", h)) + 1)
                        for k in range(2):
                            m = pe.matmul(a[:, 0:T], qx[:, 2 * h + k, t * P:(t + 1) * P], kx[:, 2 * h + k, :],
                                          start=(k == 0), stop=(k == 1), skip_group_check=True)
                        return m

                    def pv(pe, w, h=h, t=t):
                        pe.wait_ge(S("cross_out"), CROSS.index(("v", h)) + 1)
                        for d in range(2):
                            for j in range(2):
                                m = pe.matmul(bank2(2 + h % 2)[:, d, t * P:(t + 1) * P],
                                              vx[:, j, (2 * h + d) * P:(2 * h + d + 1) * P],
                                              w[:, j * P:(j + 1) * P], start=(j == 0), stop=(j == 1),
                                              skip_group_check=True)
                        return m
                    x_units.append({"n": T, "mask": None, "score": score, "pv": pv})
            xatt = Soft("xat_", x_units, 1.0 / 16.0)

            with nc.Block() as block:
                @block.sync
                def _(sp):
                    def ffn(c0, p):
                        ffn_sp(sp, c0, W[p + "_w_gu"][:, 0:DFF], W[p + "_w_gu"][:, DFF:2 * DFF], W[p + "_w_down"])
                    ffn(c_ffn1, "ffn1")
                    gemm_sp(sp, c_proj, colchunks(W["w_in"], [o for _, o, _, _ in PROJ2 + GATES]))
                    gemm_sp(sp, c_hg, colchunks(W["w_hgrn_branch"], evens))
                    gemm_sp(sp, c_att, colchunks(W["w_att_branch"], evens), 4)
                    gemm_sp(sp, c_mix, colchunks(W["w_mix_out"], evens))
                    gemm_sp(sp, c_cross, [colchunks(W["xattn_wq"] if m == "q" else W["xattn_wkv"],
                                                    [CW * c + (D if m == "v" else 0)])[0] for m, c in CROSS])
                    gemm_sp(sp, c_xo, colchunks(W["xattn_wo"], evens))
                    ffn(c_ffn2, "ffn2")
                    load_ahead(sp, 2, 1 - layer, c_ffn2 + 3 * NF)

                @block.gpsimd
                def _(pool):
                    pool.memset(hat[64:P, :, 0:64], 0.0).then_inc(S("pool_zero"), 1)

                def proj_pe(pe, n0, n1):
                    for n in range(n0, n1):
                        w = chunk(c_proj + n, KD, CW)
                        wait_chunk(pe, c_proj + n)
                        if n >= 2:
                            pe.wait_ge(S("proj_out"), n - 1)
                        for f in range(2):
                            for k in range(KD):
                                if n == 0 and f == 0:
                                    pe.wait_ge(S("mixu_in_ready"), k + 1)
                                elif n == EARLY and f == 0:
                                    pe.wait_ge(S("mix_in_ready"), k + 1)
                                a, b = ((w[:, k, f * P:(f + 1) * P], (hU if n < EARLY else hT)[:, k, :]) if PROJ2[n][2] == "F" else
                                        (hT[:, k, f * P:(f + 1) * P], w[:, k, :]))
                                m = pe.matmul(bank2(n % 2)[:, f, :], a, b, start=(k == 0), stop=(k == KD - 1))
                        m.then_inc(S("chunk_done"), 1)

                @block.tensor
                def _(pe):
                    pe.sem_inc(S("chunk_done"), RING)
                    ffn_pe(pe, "ffn1_", c_ffn1, 2, layer)
                    proj_pe(pe, 0, 1)
                    norm_pe(pe, "mix_")
                    proj_pe(pe, 1, 16)
                    def hg_maps(u):
                        h, t, hl, b = u // 2, u % 2, u // 2 % 2, 4 + u % 2
                        if u >= 2:
                            pe.wait_ge(S("hg_masked"), u - 1)
                        for c in range(2):
                            o = t * P + 64 * c
                            for l in range(7):
                                ks, qs = ((hk[:, h, o:o + 64], hq[:, h, o:o + 64]) if l == 0 else
                                          (X[:, l - 1, hl, o:o + 64], X[:, l - 1, hl, o:o + 64]))
                                pe.matmul(PS[64 * c:64 * c + 64, b, 64 * l:64 * l + 64], ks, qs, start=True,
                                          stop=True, skip_group_check=True)
                        o = t * P
                        m = pe.matmul(PS[0:64, b, 448:512], X[:, 6, hl, o:o + 64], X[:, 6, hl, o + 64:o + P],
                                      start=True, stop=True, skip_group_check=True)
                        if t == 1:
                            if u > 1:
                                pe.wait_ge(S("hg_copied"), u // 2)
                            m = pe.matmul(PS[:, 6, P * hl:P * hl + P], X[:, 7, hl, 0:P], X[:, 7, hl, P:T],
                                          start=True, stop=True, skip_group_check=True)
                        m.then_inc(S("hg_maps"), 1)

                    def hg_pv(u):
                        h, t = u // 2, u % 2
                        pe.wait_ge(S("hg_masked"), u + 1)
                        if t == 1:
                            pe.wait_ge(S("hg_copied"), u // 2 + 1)
                        if u % 4 == 0 and u:
                            pe.wait_ge(S("hg_o"), u // 4)
                        o = bank2(7)[:, h % 2, t * P:(t + 1) * P]
                        vv = hv[:, :, h * P:(h + 1) * P]
                        if t == 1:
                            pe.matmul(o, vv[:, 0, :], a128[:, h % 2, :], start=True, stop=False,
                                      skip_group_check=True)
                        pe.matmul(o, vv[:, t, :], hat[:, u % 2, :], start=(t == 0), stop=True,
                                  skip_group_check=True).then_inc(S("hg_pv"), 1)

                    pe.wait_ge(S("pool_zero"), 1)
                    for g in range(4):
                        n, u = 16 + 4 * g, 4 * g
                        pe.wait_ge(S("lev"), 16 * (g + 1))
                        hg_maps(u)
                        hg_maps(u + 1)
                        proj_pe(pe, n, n + 1)
                        hg_pv(u)
                        hg_maps(u + 2)
                        hg_pv(u + 1)
                        hg_maps(u + 3)
                        proj_pe(pe, n + 1, n + 2)
                        hg_pv(u + 2)
                        hg_pv(u + 3)
                        proj_pe(pe, n + 2, n + 4)
                    proj_pe(pe, 32, 33)
                    pe.wait_ge(S("hg_sq"), 1)
                    for b in range(4):
                        pe.matmul(bank(HG_SUMS[b]), ones[:], Xf[:, 512 * b:512 * b + 512], start=True, stop=True)\
                          .then_inc(S("hg_sum"), 1)
                    proj_pe(pe, 33, 34)
                    pe.wait_ge(S("rope"), 12)

                    def gates(u):
                        if u < 8:
                            pe.wait_ge(S("proj_out"), 33 + u)
                            gemm_pe1(pe, c_gate + u, u % 2, hT)
                        if u == 0:
                            pe.wait_ge(S("hg_root"), 4)
                    soft_pe(pe, att, {}, gates)
                    pe.wait_ge(S("hg_done"), 1)
                    for n in range(8):
                        if n < 2:
                            pe.wait_ge(S("proj_out"), 41 + n)
                        else:
                            pe.wait_ge(S("branch_out"), n - 1)
                        if n == 4:
                            pe.wait_ge(S("att_o_out"), 2)
                        gemm_pe1(pe, c_hg + n, n % 2, hq if n < 4 else yat, "F", KD if n < 4 else 4)
                    pe.wait_ge(S("branch_out"), 8)
                    gemm_pe(pe, c_mix, "FFFF", mg)
                    def cross_pe(n):
                        m = CROSS[n][0]
                        if n < 2:
                            pe.wait_ge(S("mixo_x_ready"), n + 1)
                        else:
                            pe.wait_ge(S("cross_out"), n - 1)
                        gemm_pe1(pe, c_cross + n, n % 2, hT if m == "q" else memn, "T" if m == "v" else "F")

                    def cross_fill(u):
                        if u in CROSS_FILL:
                            cross_pe(CROSS_FILL[u])
                    pe.wait_ge(S("mem_in_ready"), 8)
                    cross_pe(0)
                    norm_pe(pe, "xa_")
                    for n in range(1, CROSS_AHEAD):
                        if CROSS[n] == ("q", 0):
                            pe.wait_ge(S("xa_in_ready"), 8)
                        cross_pe(n)
                    soft_pe(pe, xatt, {4: 1, 6: 2}, cross_fill)
                    pe.wait_ge(S("xat_o_out"), 4)
                    gemm_pe(pe, c_xo, "FFFF", ox)
                    ffn_pe(pe, "ffn2_", c_ffn2, 2, layer)

                def proj_act(act, n0, n1):
                    for n in range(n0, n1):
                        name, _, _, c = PROJ2[n]
                        src = bank2(n % 2)
                        act.wait_ge(S("chunk_done"), RING + c_proj + n + 1)
                        if name in ("aq", "ak"):
                            r = c + (6 if name == "ak" else 0)
                            if r >= 2:
                                act.wait_ge(S("rope"), r - 1)
                            act.activation(rp[:, r % 2, 0], src, ACT.Copy)
                            act.activation(rp[0:64, r % 2, 1], src[64:128], ACT.Copy, scale=-1.0)
                            m = act.activation(rp[64:128, r % 2, 1], src[0:64], ACT.Copy)
                        elif name in ("i", "av"):
                            m = act.activation({"i": hv, "av": av}[name][:, :, CW * c:CW * (c + 1)], src, ACT.Copy)
                        else:
                            dst, f, s = {"f": (hP, ACT.Sigmoid, 1.0), "q": (hq, ACT.Copy, float(P) ** -0.5),
                                         "og": (hog, ACT.Silu, 1.0)}[name]
                            if n < EARLY:
                                act.wait_ge(S("early_out"), n + 1)
                                src = dst[:, 2 * c:2 * c + 2, :]
                            m = act.activation(dst[:, 2 * c:2 * c + 2, :], src, f, scale=s)
                        m.then_inc(S("proj_out"), 1)

                @block.scalar
                def _(act):
                    st = Step(act, S("act_step"))
                    ffn_act_all(act, "ffn1_", c_ffn1, None)
                    norm_act(act, "mix_", xT, S("ffn1_x_ready"))
                    proj_act(act, 0, 8)
                    act.wait_ge(S("f_split"), 1)
                    act.activation(xa, xa, ACT.Ln).then_inc(S("f_ln"), 1)
                    act.activation(xb, xb, ACT.Ln).then_inc(S("f_ln"), 1)
                    proj_act(act, 8, 12)

                    def decays(g, l0, l1):
                        for l in range(l0, l1):
                            act.wait_ge(S("pre"), 8 * g + l + 1)
                            act.activation(X[:, l], X[:, l], ACT.Exp).then_inc(S("lev_exp"), 1)

                    def cross(u):
                        act.wait_ge(S("hg_maps"), u + 1)
                        if u >= 4:
                            act.wait_ge(S("hg_pv"), u - 3)
                        act.activation(a128[:, u // 2 % 2, :], PS[:, 6, P * (u // 2 % 2):P * (u // 2 % 2) + P],
                                       ACT.Copy).then_inc(S("hg_copied"), 1)
                    for j in range(4):
                        decays(0, 2 * j, 2 * j + 2)
                        proj_act(act, 12 + j, 13 + j)
                    for g in range(4):
                        n, u = 16 + 4 * g, 4 * g
                        cross(u + 1)
                        proj_act(act, n, n + 1)
                        cross(u + 3)
                        if g < 3:
                            decays(g + 1, 0, 4)
                        proj_act(act, n + 1, n + 2)
                        act.wait_ge(S("hg_pv"), u + 4)
                        act.activation(hq[:, 2 * g:2 * g + 2, :], bank2(7), ACT.Copy).then_inc(S("hg_o"), 1)
                        if g < 3:
                            decays(g + 1, 4, 8)
                        proj_act(act, n + 2, n + 4)
                    act.wait_ge(S("hg_o"), 4)
                    act.activation(xa, hq, ACT.Square).then_inc(S("hg_sq"), 1)
                    proj_act(act, 32, 33)
                    for b in range(4):
                        act.wait_ge(S("hg_sum"), b + 1)
                        act.activation(Xf[:, 2048 + 512 * b:2560 + 512 * b], bank(HG_SUMS[b]), ACT.Sqrt, scale=1.0 / P,
                                       bias=epst[:, 0:1]).then_inc(S("hg_root"), 1)
                    proj_act(act, 33, 34)

                    def gates(u):
                        if 1 <= u < 9:
                            n = u - 1
                            act.wait_ge(S("chunk_done"), RING + c_gate + n + 1)
                            act.activation((sgB, sgA)[n // 4][:, 2 * (n % 4):2 * (n % 4) + 2, :], bank2(n % 2),
                                           ACT.Sigmoid).then_inc(S("proj_out"), 1)
                    soft_act(act, att, {3: (yat[:, 0:2, :], bank2(2)), 7: (yat[:, 2:4, :], bank2(3))}, gates)

                    def cross_act(n):
                        m, c = CROSS[n]
                        act.wait_ge(S("chunk_done"), RING + c_cross + n + 1)
                        dst = vx[:, :, CW * c:CW * (c + 1)] if m == "v" else (kx, qx)[m == "q"][:, 2 * c:2 * c + 2, :]
                        act.activation(dst, bank2(n % 2), ACT.Copy).then_inc(S("cross_out"), 1)

                    def cross_evac(u):
                        if u in CROSS_FILL:
                            cross_act(CROSS_FILL[u])
                    norm_act(act, "xa_", xT, S("mixo_x_ready"))
                    for n in range(CROSS_AHEAD):
                        cross_act(n)
                    soft_act(act, xatt, {2 * h + 1: (ox[:, 2 * h:2 * h + 2, :], bank2(2 + h % 2)) for h in range(4)},
                             cross_evac)
                    ffn_act_all(act, "ffn2_", c_ffn2, S("xo_x_ready"))

                def rope_dve(dve, st, r0, r1):
                    for r in range(r0, r1):
                        dve.wait_ge(S("proj_out"), idx[("aq", "ak")[r // 6], r % 6] + 1)
                        raw, swp = rp[:, r % 2, 0], rp[:, r % 2, 1]
                        dst = (aq, ak)[r // 6][:, 2 * (r % 6):2 * (r % 6) + 2, :]
                        st.link(dve.tensor_tensor(raw, raw, over(cosT, 2), ALU.mult))
                        st.then(dve.tensor_tensor(swp, swp, over(sinT, 2), ALU.mult))
                        dve.tensor_tensor(dst, raw, swp, ALU.add).then_inc(S("rope"), 1)

                @block.vector
                def _(dve):
                    st = Step(dve, S("dve_step"))
                    dve.tensor_copy(pcol[:, 0:NROW2].unsqueeze(1), cols2[:, bass.ds(layer, 1), :])\
                       .then_inc(S("cols"), 1)
                    dve.wait_ge(S("cols"), 1)
                    st.then(dve.tensor_copy(lbc[:, 0:1, :], lb01[:, bass.ds(layer, 1), :]))
                    st.then(dve.tensor_scalar(lbc[:, 1, :], lbc[:, 0, :], -1.0, 1.0, ALU.mult, ALU.add))
                    ffn_dve_all(dve, "ffn1_", c_ffn1, COL2["ffn1_norm_2"], None)
                    scaled_dve(dve, "mixu_", hU, xT, COL2["mix_norm_2"], False, S("ffn1_x_ready"))
                    norm_dve(dve, "mix_")
                    scaled_dve(dve, "mix_", hT, xT, COL2["mix_norm_2"], True)
                    early_out_dve(dve, c_proj, [hP[:, 2 * n:2 * n + 2, :] for n in range(EARLY)])
                    dve.wait_ge(S("proj_out"), 4)
                    for k in range(KD):
                        m = dve.tensor_scalar(hP[:, k, :], hP[:, k, :], lbc[:, 1, k:k + 1], lbc[:, 0, k:k + 1],
                                              ALU.mult, ALU.add)
                    st.then(m)
                    st.link(dve.tensor_scalar(hk, hP, -1.0, 1.0, ALU.mult, ALU.add))
                    st.link(dve.tensor_scalar(xa, hP, 2.0 ** -60, None, ALU.max))
                    dve.tensor_scalar(xb, hP, 2.0 ** -60, 2.0 ** 60, ALU.min, ALU.mult).then_inc(S("f_split"), 1)
                    dve.wait_ge(S("f_ln"), 2)
                    st.then(dve.tensor_tensor(hP, xa, xb, ALU.add))
                    dve.wait_ge(S("proj_out"), 8)
                    def before(g):
                        pr = hP[:, 2 * g:2 * g + 2, :]
                        if g:
                            dve.wait_ge(S("hg_maps"), 4 * g)
                        for l, m in enumerate(LEVELS):
                            first, second = halves(pr, m)
                            xf, xs_ = halves(X[:, l], m)
                            dve.tensor_tensor(xf, last_of(first, m), first, ALU.subtract)
                            dve.tensor_copy(xs_, second).then_inc(S("pre"), 1)
                            dve.wait_ge(S("pre"), 8 * g + l + 1)
                            if m < P:
                                st.then(dve.tensor_tensor(second, second, last_of(first, m), ALU.add))

                    def decayed(g):
                        for l, m in enumerate(LEVELS):
                            dve.wait_ge(S("lev_exp"), 8 * g + l + 1)
                            for half in range(2):
                                xh = halves(X[:, l], m)[half]
                                qk = halves((hk, hq)[half][:, 2 * g:2 * g + 2, :], m)[half]
                                dve.tensor_tensor(xh, xh, qk, ALU.mult).then_inc(S("lev"), 1)

                    def masked(u):
                        dve.wait_ge(S("hg_maps"), u + 1)
                        st.then(dve.tensor_tensor(mt[:, u % 2], PS[:, 4 + u % 2, 0:448]
                                                  .rearrange("p (l n) -> p l n", l=7), lmask, ALU.mult))
                        if u >= 2:
                            dve.wait_ge(S("hg_pv"), u - 1)
                        for c in range(2):
                            q = slice(64 * c, 64 * c + 64)
                            dve.tensor_reduce(hat[q, u % 2, q], mt[q, u % 2].rearrange("p l n -> p n l"), AX,
                                              ALU.add)
                        dve.tensor_copy(hat[0:64, u % 2, 64:P], PS[0:64, 4 + u % 2, 448:512])\
                           .then_inc(S("hg_masked"), 1)

                    before(0)
                    decayed(0)
                    for g in range(4):
                        u = 4 * g
                        masked(u)
                        masked(u + 1)
                        masked(u + 2)
                        rope_dve(dve, st, 3 * g, 3 * g + 1)
                        masked(u + 3)
                        if g < 3:
                            before(g + 1)
                        rope_dve(dve, st, 3 * g + 1, 3 * g + 2)
                        if g < 3:
                            decayed(g + 1)
                        rope_dve(dve, st, 3 * g + 2, 3 * g + 3)
                    def hg_output(u):
                        if u == 0:
                            dve.wait_ge(S("hg_root"), 4)
                            st.then(dve.reciprocal(xb, xb))
                        elif u == 1:
                            for k in range(KD):
                                gc = COL2["hgrn_head_norm_2"] + k
                                m = dve.scalar_tensor_tensor(hq[:, k, :], hq[:, k, :], pcol[:, gc:gc + 1],
                                                             xb[:, k, :], ALU.mult, ALU.mult)
                            st.then(m)
                        elif u == 2:
                            dve.wait_ge(S("proj_out"), 16)
                            dve.tensor_tensor(hq, hq, hog, ALU.mult).then_inc(S("hg_done"), 1)
                    soft_dve(dve, st, att, hg_output)
                    for k in range(KD):
                        gc = COL2["mem_norm_2"] + k
                        dve.scalar_tensor_tensor(memn[:, k, :], memT[:, k, :], pcol[:, gc:gc + 1], rmem, ALU.mult,
                                                 ALU.mult).then_inc(S("mem_in_ready"), 1)
                    dve.wait_ge(S("proj_out"), 42)
                    for n in range(8):
                        dve.wait_ge(S("chunk_done"), RING + c_hg + n + 1)
                        c = n % 4
                        m2 = mg[:, 2 * c:2 * c + 2, :]
                        if n < 4:
                            dve.tensor_tensor(m2, bank2(n % 2), sgB[:, 2 * c:2 * c + 2, :], ALU.mult)\
                               .then_inc(S("branch_out"), 1)
                        else:
                            dve.wait_ge(S("branch_out"), n)
                            st.then(dve.tensor_tensor(brt, bank2(n % 2), sgA[:, 2 * c:2 * c + 2, :], ALU.mult))
                            dve.tensor_tensor(m2, m2, brt, ALU.add).then_inc(S("branch_out"), 1)
                    residual_dve(dve, "mixo_", c_mix)
                    norm_dve(dve, "xa_")
                    scaled_dve(dve, "xa_", hT, xT, COL2["xattn_norm_2"], True)
                    soft_dve(dve, st, xatt, lambda u: None)
                    residual_dve(dve, "xo_", c_xo)
                    ffn_dve_all(dve, "ffn2_", c_ffn2, COL2["ffn2_norm_2"], S("xo_x_ready"))

            clear_signals()
        end_part()

        with nc.Block() as block:
            rows = sq[:].rearrange("p k t -> p (k t)").rearrange("p (a n) -> p a n", a=TT)

            @block.sync
            def _(sp):
                sp.dma_start(prow[0:8, :], A["final_norm_2"].rearrange("(k p) -> k p", p=P)).then_inc(S("rows"), 16)
                for j in range(2):
                    sp.wait_ge(ahead[2][j], 16 * (DEPTH + 1))
                sp.wait_ge(S("rows_out"), 4)
                sp.dma_start(out[0].rearrange("(a p) n -> p a n", p=P), rows).then_inc(S("stored"), 16)
                sp.wait_ge(S("stored"), 16)

            @block.scalar
            def _(act):
                norm_act(act, "fin_", xT)

            @block.tensor
            def _(pe):
                pe.wait_ge(S("rows"), 16)
                pe.transpose(bank(0, 8), prow[0:8, :], ident[0:8, 0:8]).then_inc(S("cols_turn"), 1)
                norm_pe(pe, "fin_")
                for a in range(TT):
                    for k in range(KD):
                        if a == 0:
                            pe.wait_ge(S("fin_in_ready"), k + 1)
                        m = pe.transpose(PS[:, 2 * a + k // 4, (k % 4) * P:(k % 4 + 1) * P],
                                         hT[:, k, a * P:(a + 1) * P], ident[:])
                        if k % 4 == 3:
                            m.then_inc(S("row_turn"), 1)

            @block.vector
            def _(dve):
                dve.wait_ge(S("cols_turn"), 1)
                dve.tensor_copy(pcol[:, 0:8], bank(0, 8)).then_inc(S("cols"), 1)
                dve.wait_ge(S("cols"), 1)
                norm_dve(dve, "fin_")
                scaled_dve(dve, "fin_", hT, xT, 0, True)
                for j in range(4):
                    dve.wait_ge(S("row_turn"), j + 1)
                    dve.tensor_copy(rows[:, j // 2, 512 * (j % 2):512 * (j % 2) + 512], bank(j))\
                       .then_inc(S("rows_out"), 1)
        end_part()


_INS = ['x', 'ffn1_norm', 'ffn1_w_gate', 'ffn1_w_up', 'ffn1_w_down', 'mix_norm', 'w_in', 'gla_w_gate_up',
        'gla_b_gate', 'gla_norm', 'fox_b_forget', 'fox_q_norm', 'fox_k_norm', 'fox_out_norm', 'ssm_conv_w',
        'ssm_conv_b', 'ssm_dt_bias', 'ssm_A_log', 'ssm_D', 'ssm_norm', 'sc_conv_w', 'sc_out_norm', 'w_out',
        'ffn2_norm', 'ffn2_w_gate', 'ffn2_w_up', 'ffn2_w_down', 'mem_2', 'positions_2', 'ffn1_norm_2',
        'ffn1_w_gu_2', 'ffn1_w_down_2', 'mix_norm_2', 'w_in_2', 'hgrn_lower_bounds_2', 'hgrn_head_norm_2',
        'w_att_branch_2', 'w_hgrn_branch_2', 'w_mix_out_2', 'xattn_norm_2', 'mem_norm_2', 'xattn_wq_2',
        'xattn_wkv_2', 'xattn_wo_2', 'ffn2_norm_2', 'ffn2_w_gu_2', 'ffn2_w_down_2', 'final_norm_2']
_OUTS = [((1, T, D), 'float32')]


def kernel(**inputs):
    import numpy as _np
    import concourse.bacc as _bacc
    from concourse import mybir as _mybir
    from concourse.bass_utils import run_bass_kernel_spmd as _run

    nc = _bacc.Bacc("TRN2", target_bir_lowering=False, num_devices=1)
    arrays, args = {}, {}
    inv = (_np.float32(10000.0) ** (-_np.arange(0, P, 2, dtype=_np.float32) / _np.float32(P))).astype(_np.float32)
    consts = {"inv_freq": _np.concatenate([inv, inv])}
    for name in _INS + ["inv_freq"]:
        a = _np.ascontiguousarray(consts[name] if name in consts else inputs[name])
        arrays[f"in_{name}_dram"] = a
        args[name] = nc.dram_tensor(f"in_{name}_dram", a.shape, _mybir.dt.from_np(a.dtype),
                                    kind="ExternalInput").ap()
    (shape, dtype), = _OUTS
    out = nc.dram_tensor("out_0_dram", shape, _mybir.dt.from_np(_np.dtype(dtype)), kind="ExternalOutput").ap()
    build(nc, args, out)
    r = _run(nc, [arrays], core_ids=[0])
    return r.results[0]["out_0_dram"]
```
